# Optimizing a Trainium2 kernel written in Bass

```python
import jax, jax.numpy as jnp
from jax import lax
import numpy as np

D_MODEL = 1024
BATCH = 1
SEQ = 1024
DEPTH = 1
DEC_BATCH = 8
DEC_SEQ = 16
PAST_LEN = 256

CHUNK = 64
HEAD_DIM = 64
ATTN_SCALE = HEAD_DIM ** -0.5
NEG_INF = -1e30
EPS = 1e-6
A_HEADS = 8
A_WIDTH = A_HEADS * HEAD_DIM
A_BACK_CHUNKS = 8
A_PAST = A_BACK_CHUNKS * CHUNK
A_BAND = (A_BACK_CHUNKS + 1) * CHUNK
REL_CLIP = 256
REL_SIZE = (CHUNK - 1) + REL_CLIP + 1
B_HEADS = 8
B_KV_HEADS = 2
B_GROUP = B_HEADS // B_KV_HEADS
B_WIDTH = B_HEADS * HEAD_DIM
B_KV_WIDTH = B_KV_HEADS * HEAD_DIM
B_WINDOW = 128
B_BACK_CHUNKS = B_WINDOW // CHUNK
B_PAST = B_BACK_CHUNKS * CHUNK
B_BAND = (B_BACK_CHUNKS + 1) * CHUNK
MIX_WIDTH = A_WIDTH + B_WIDTH
IN_WIDTH = 3 * A_WIDTH + B_WIDTH + 2 * B_KV_WIDTH
PEER_HEADS = 8
N_KEYS = 128
N_EXPERTS = N_KEYS * N_KEYS
PEER_TOPK = 16
D_KEY = 256
D_HALF = D_KEY // 2
PEER_BLOCK = 128

kernel_name = "hymba_chunk_band_swa_peer_stream_step"

def rms_norm(x, g):
    xf = x.astype(jnp.float32)
    y = xf * lax.rsqrt(jnp.mean(xf * xf, axis=-1, keepdims=True) + EPS)
    return (y * g.astype(jnp.float32)).astype(x.dtype)

def project(hn, w_in):
    z = hn @ w_in
    cuts = [A_WIDTH, 2 * A_WIDTH, 3 * A_WIDTH, 3 * A_WIDTH + B_WIDTH,
            3 * A_WIDTH + B_WIDTH + B_KV_WIDTH]
    qa, ka, va, qb, kb, vb = jnp.split(z, cuts, axis=-1)
    lead = hn.shape[:-1]
    return (qa.reshape(*lead, A_HEADS, HEAD_DIM),
            ka.reshape(*lead, A_HEADS, HEAD_DIM),
            va.reshape(*lead, A_HEADS, HEAD_DIM),
            qb.reshape(*lead, B_KV_HEADS, B_GROUP, HEAD_DIM),
            kb.reshape(*lead, B_KV_HEADS, HEAD_DIM),
            vb.reshape(*lead, B_KV_HEADS, HEAD_DIM))

def chunk_band(t, n_back):
    b, s = t.shape[:2]
    nc = s // CHUNK
    pad = [(0, 0), (n_back * CHUNK, 0)] + [(0, 0)] * (t.ndim - 2)
    tc = jnp.pad(t, pad).reshape(b, nc + n_back, CHUNK, *t.shape[2:])
    return jnp.concatenate([tc[:, j:j + nc] for j in range(n_back + 1)], axis=2)

def band_valid(nc, n_back):
    kc = jnp.arange(nc)[:, None] - n_back + jnp.arange((n_back + 1) * CHUNK)[None, :] // CHUNK
    return kc >= 0

def band_mask(qpos, kpos, n_back):
    qc = qpos[:, None] // CHUNK
    kc = kpos[None, :] // CHUNK
    return (kc <= qc) & (kc >= qc - n_back)

def rel_pos_bias(rel_bias, dist):
    idx = jnp.clip(dist, -(CHUNK - 1), REL_CLIP) + (CHUNK - 1)
    return rel_bias[:, idx].astype(jnp.float32)

def alibi_bias(dist):
    slopes = 2.0 ** (-(8.0 / B_HEADS) * jnp.arange(1, B_HEADS + 1, dtype=jnp.float32))
    return -slopes[:, None, None] * jnp.abs(dist).astype(jnp.float32)[None]

def sink_softmax(scores, sinks):
    s = sinks.astype(jnp.float32)[:, None, None]
    m = jnp.maximum(jnp.max(scores, axis=-1, keepdims=True), s)
    e = jnp.exp(scores - m)
    return e / (jnp.sum(e, axis=-1, keepdims=True) + jnp.exp(s - m))

def sample_positions(t, l):
    qpos = PAST_LEN + jnp.arange(t)
    kpos = jnp.concatenate([PAST_LEN - l + jnp.arange(l), qpos])
    return qpos, kpos

def attn_a_prompt(q, k, v, rel_bias):
    b, s = q.shape[:2]
    nc = s // CHUNK
    qc = q.reshape(b, nc, CHUNK, A_HEADS, HEAD_DIM)
    kband = chunk_band(k, A_BACK_CHUNKS)
    vband = chunk_band(v, A_BACK_CHUNKS)
    sc = jnp.einsum('bcqhd,bckhd->bchqk', qc, kband,
                    preferred_element_type=jnp.float32) * ATTN_SCALE
    dist = A_PAST + jnp.arange(CHUNK)[:, None] - jnp.arange(A_BAND)[None, :]
    sc = sc + rel_pos_bias(rel_bias, dist)
    valid = band_valid(nc, A_BACK_CHUNKS)
    sc = jnp.where(valid[None, :, None, None, :], sc, NEG_INF)
    p = jax.nn.softmax(sc, axis=-1).astype(v.dtype)
    o = jnp.einsum('bchqk,bckhd->bcqhd', p, vband)
    return o.reshape(b, s, A_WIDTH)

def attn_b_prompt(q, k, v, sinks):
    b, s = q.shape[:2]
    nc = s // CHUNK
    qc = q.reshape(b, nc, CHUNK, B_KV_HEADS, B_GROUP, HEAD_DIM)
    kband = chunk_band(k, B_BACK_CHUNKS)
    vband = chunk_band(v, B_BACK_CHUNKS)
    sc = jnp.einsum('bcqngd,bcsnd->bcngqs', qc, kband,
                    preferred_element_type=jnp.float32) * ATTN_SCALE
    sc = sc.reshape(b, nc, B_HEADS, CHUNK, B_BAND)
    dist = B_PAST + jnp.arange(CHUNK)[:, None] - jnp.arange(B_BAND)[None, :]
    sc = sc + alibi_bias(dist)
    valid = band_valid(nc, B_BACK_CHUNKS)
    sc = jnp.where(valid[None, :, None, None, :], sc, NEG_INF)
    p = sink_softmax(sc, sinks).reshape(b, nc, B_KV_HEADS, B_GROUP, CHUNK, B_BAND)
    o = jnp.einsum('bcngqs,bcsnd->bcqngd', p.astype(v.dtype), vband)
    return o.reshape(b, s, B_WIDTH)

def attn_a_sample(q, k, v, ck, cv, rel_bias):
    b, t = q.shape[:2]
    l = ck.shape[1]
    kk = jnp.concatenate([ck.astype(k.dtype), k], axis=1)
    vv = jnp.concatenate([cv.astype(v.dtype), v], axis=1)
    qpos, kpos = sample_positions(t, l)
    dist = qpos[:, None] - kpos[None, :]
    sc = jnp.einsum('bqhd,bkhd->bhqk', q, kk,
                    preferred_element_type=jnp.float32) * ATTN_SCALE
    sc = sc + rel_pos_bias(rel_bias, dist)[None]
    sc = jnp.where(band_mask(qpos, kpos, A_BACK_CHUNKS)[None, None], sc, NEG_INF)
    p = jax.nn.softmax(sc, axis=-1).astype(v.dtype)
    o = jnp.einsum('bhqk,bkhd->bqhd', p, vv)
    return o.reshape(b, t, A_WIDTH)

def attn_b_sample(q, k, v, ck, cv, sinks):
    b, t = q.shape[:2]
    l = ck.shape[1]
    kk = jnp.concatenate([ck.astype(k.dtype), k], axis=1)
    vv = jnp.concatenate([cv.astype(v.dtype), v], axis=1)
    qpos, kpos = sample_positions(t, l)
    dist = qpos[:, None] - kpos[None, :]
    sc = jnp.einsum('bqngd,bsnd->bngqs', q, kk,
                    preferred_element_type=jnp.float32) * ATTN_SCALE
    sc = sc.reshape(b, B_HEADS, t, l + t) + alibi_bias(dist)[None]
    sc = jnp.where(band_mask(qpos, kpos, B_BACK_CHUNKS)[None, None], sc, NEG_INF)
    p = sink_softmax(sc, sinks).reshape(b, B_KV_HEADS, B_GROUP, t, l + t)
    o = jnp.einsum('bngqs,bsnd->bqngd', p.astype(v.dtype), vv)
    return o.reshape(b, t, B_WIDTH)

def merge_heads(oa, ob, ga, gb, w_out):
    return jnp.concatenate([rms_norm(oa, ga), rms_norm(ob, gb)], axis=-1) @ w_out

def peer_ffn(xn, w_query, sub_keys, expert_u, expert_v):
    shape = xn.shape
    xt = xn.reshape(-1, D_MODEL)
    n = xt.shape[0]
    nb = -(-n // PEER_BLOCK)
    xt = jnp.pad(xt, ((0, nb * PEER_BLOCK - n), (0, 0))).reshape(nb, PEER_BLOCK, D_MODEL)

    def block(xb):
        q = (xb @ w_query).reshape(PEER_BLOCK, PEER_HEADS, 2, D_HALF)
        s = jnp.einsum('thpd,hpkd->thpk', q, sub_keys,
                       preferred_element_type=jnp.float32)
        sv, si = lax.top_k(s, PEER_TOPK)
        cand = sv[:, :, 0, :, None] + sv[:, :, 1, None, :]
        cidx = si[:, :, 0, :, None] * N_KEYS + si[:, :, 1, None, :]
        cand = cand.reshape(PEER_BLOCK, PEER_HEADS, PEER_TOPK * PEER_TOPK)
        cidx = cidx.reshape(PEER_BLOCK, PEER_HEADS, PEER_TOPK * PEER_TOPK)
        fv, fi = lax.top_k(cand, PEER_TOPK)
        eidx = jnp.take_along_axis(cidx, fi, axis=-1)
        g = jax.nn.softmax(fv, axis=-1)
        u = expert_u[eidx]
        a = jnp.einsum('thkd,td->thk', u, xb, preferred_element_type=jnp.float32)
        w = (g * jax.nn.gelu(a, approximate=False)).astype(xb.dtype)
        return jnp.einsum('thk,thkd->td', w, expert_v[eidx])

    out = lax.map(block, xt).reshape(nb * PEER_BLOCK, D_MODEL)[:n]
    return out.reshape(shape)

def setup_inputs(seed: int = 0) -> dict:
    key = jax.random.key(seed)
    ks = jax.random.split(key, 20)
    f32 = jnp.float32
    la = min(A_PAST, PAST_LEN)
    lb = min(B_WINDOW, PAST_LEN)

    def nrm(k, shape, scale):
        return jax.random.normal(k, shape, f32) * scale

    return {
        "x_prompt": nrm(ks[0], (BATCH, SEQ, D_MODEL), 1.0),
        "x_sample": nrm(ks[1], (DEC_BATCH, DEC_SEQ, D_MODEL), 1.0),
        "cache_a_k": nrm(ks[2], (DEPTH, DEC_BATCH, la, A_HEADS, HEAD_DIM), 1.0),
        "cache_a_v": nrm(ks[3], (DEPTH, DEC_BATCH, la, A_HEADS, HEAD_DIM), 1.0),
        "cache_b_k": nrm(ks[4], (DEPTH, DEC_BATCH, lb, B_KV_HEADS, HEAD_DIM), 1.0),
        "cache_b_v": nrm(ks[5], (DEPTH, DEC_BATCH, lb, B_KV_HEADS, HEAD_DIM), 1.0),
        "norm1_g": 1.0 + nrm(ks[6], (DEPTH, D_MODEL), 0.02),
        "w_in": nrm(ks[7], (DEPTH, D_MODEL, IN_WIDTH), D_MODEL ** -0.5),
        "rel_bias": nrm(ks[8], (DEPTH, A_HEADS, REL_SIZE), 0.1),
        "sinks": nrm(ks[9], (DEPTH, B_HEADS), 0.5),
        "out_norm_a_g": 1.0 + nrm(ks[10], (DEPTH, A_WIDTH), 0.02),
        "out_norm_b_g": 1.0 + nrm(ks[11], (DEPTH, B_WIDTH), 0.02),
        "w_out": nrm(ks[12], (DEPTH, MIX_WIDTH, D_MODEL), MIX_WIDTH ** -0.5),
        "norm2_g": 1.0 + nrm(ks[13], (DEPTH, D_MODEL), 0.02),
        "w_query": nrm(ks[14], (DEPTH, D_MODEL, PEER_HEADS * D_KEY), D_MODEL ** -0.5),
        "sub_keys": nrm(ks[15], (DEPTH, PEER_HEADS, 2, N_KEYS, D_HALF), D_HALF ** -0.5),
        "expert_u": nrm(ks[16], (DEPTH, N_EXPERTS, D_MODEL), D_MODEL ** -0.5),
        "expert_v": nrm(ks[17], (DEPTH, N_EXPERTS, D_MODEL), PEER_HEADS ** -0.5),
        "norm_f_g": 1.0 + nrm(ks[18], (D_MODEL,), 0.02),
    }

def reference(x_prompt, x_sample, cache_a_k, cache_a_v, cache_b_k, cache_b_v,
              norm1_g, w_in, rel_bias, sinks, out_norm_a_g, out_norm_b_g, w_out,
              norm2_g, w_query, sub_keys, expert_u, expert_v, norm_f_g):
    hp = x_prompt
    hs = x_sample
    la_p = min(A_PAST, x_prompt.shape[1])
    lb_p = min(B_WINDOW, x_prompt.shape[1])
    ak_p, av_p, bk_p, bv_p = [], [], [], []
    ak_s, av_s, bk_s, bv_s = [], [], [], []
    for l in range(DEPTH):
        qa, ka, va, qb, kb, vb = project(rms_norm(hp, norm1_g[l]), w_in[l])
        oa = attn_a_prompt(qa, ka, va, rel_bias[l])
        ob = attn_b_prompt(qb, kb, vb, sinks[l])
        hp = hp + merge_heads(oa, ob, out_norm_a_g[l], out_norm_b_g[l], w_out[l])
        hp = hp + peer_ffn(rms_norm(hp, norm2_g[l]), w_query[l], sub_keys[l],
                           expert_u[l], expert_v[l])
        ak_p.append(ka[:, -la_p:])
        av_p.append(va[:, -la_p:])
        bk_p.append(kb[:, -lb_p:])
        bv_p.append(vb[:, -lb_p:])
        qa, ka, va, qb, kb, vb = project(rms_norm(hs, norm1_g[l]), w_in[l])
        oa = attn_a_sample(qa, ka, va, cache_a_k[l], cache_a_v[l], rel_bias[l])
        ob = attn_b_sample(qb, kb, vb, cache_b_k[l], cache_b_v[l], sinks[l])
        hs = hs + merge_heads(oa, ob, out_norm_a_g[l], out_norm_b_g[l], w_out[l])
        hs = hs + peer_ffn(rms_norm(hs, norm2_g[l]), w_query[l], sub_keys[l],
                           expert_u[l], expert_v[l])
        ak_s.append(ka)
        av_s.append(va)
        bk_s.append(kb)
        bv_s.append(vb)
    y_prompt = rms_norm(hp, norm_f_g)
    y_sample = rms_norm(hs, norm_f_g)
    return (y_prompt, y_sample,
            jnp.stack(ak_p), jnp.stack(av_p), jnp.stack(bk_p), jnp.stack(bv_p),
            jnp.stack(ak_s), jnp.stack(av_s), jnp.stack(bk_s), jnp.stack(bv_s))


_drawn_inputs = setup_inputs


def setup_inputs(seed=0):
    import zlib

    import numpy as np

    out = dict(_drawn_inputs(seed))
    spreads = {}
    factors = {'out_norm_a_g': 9.629, 'out_norm_b_g': 9.61, 'norm2_g': 8.95, 'norm_f_g': 8.414}
    for name, (base, spread) in spreads.items():
        noise = np.random.default_rng([zlib.crc32(name.encode()), seed]).standard_normal(out[name].shape)
        drawn = base * np.exp(spread * noise) if base else spread * noise
        out[name] = __import__('jax').numpy.asarray(drawn.astype(out[name].dtype))
    for name, factor in factors.items():
        out[name] = (out[name] * factor).astype(out[name].dtype)
    return out
```

```python
import concourse.bass as bass
from concourse import mybir
from concourse.alu_op_type import AluOpType as ALU
from contextlib import ExitStack

F32 = mybir.dt.float32
U32 = mybir.dt.uint32
ACT = mybir.ActivationFunctionType
AX_X = mybir.AxisListType.X

P = 128
D = 1024
KD = D // P
HD = 64
H = 8
AW = H * HD
NT_PROMPT = 8
NT = 9
W_IN = 3 * AW + AW + 4 * HD
A_BLK = 5
A_KEYS = A_BLK * P
B_KEYS = 2 * P
STREAMS = 8
FR = 16
CA = 256
CB = 128
EPS = 1e-6
SCALE = HD ** -0.5
NEG = -1e30
LOWEST = -3.0e38
NKEYS = 128
TOPK = 16
ROWS = [TOPK // (i + 1) for i in range(TOPK)]
CAND = sum(ROWS)
SLOTS = H * TOPK
RING = 8
GROUP = 4
QSP = 2
PARTS = H
CREDIT = 1


class Chain:

    def __init__(self, eng, sem):
        self.eng, self.sem, self.n = eng, sem, 0

    def restart(self):
        self.settle()
        self.eng.sem_clear(self.sem)
        self.n = 0

    def mark(self, ins):
        ins.then_inc(self.sem, 1)
        self.n += 1

    def pass_on(self):
        self.eng.sem_inc(self.sem, 1)
        self.n += 1
        self.settle()

    def settle(self):
        self.eng.wait_ge(self.sem, self.n)




def build(nc, ins, outs):
    (x_prompt, x_sample, ckT, cv, ckbT, cvb, g1, w_in, bias_a, bias_b, bias_sa, bias_sb, sinks, sink_rows,
     g_ab, w_out, g2, w_query, subk, experts, gf) = ins
    (y_p, y_s, ak_p, av_p, bk_p, bv_p, ak_s, av_s, bk_s, bv_s) = outs
    h_dram = nc.dram_tensor("h_scratch", (NT * P, D), F32, kind="Internal").ap()

    ctx = ExitStack()
    with ctx:
        def sem(name):
            return ctx.enter_context(nc.semaphore(name))

        PS = ctx.enter_context(nc.psum_tensor("PS", [P, 8, 512], F32))
        ident_t = ctx.enter_context(nc.sbuf_tensor("ident", [P, P], F32))
        ident = ident_t[:, :]
        eps = ctx.enter_context(nc.sbuf_tensor("eps", [P, 1], F32))[:, :]
        arena_t = ctx.enter_context(nc.sbuf_tensor("arena", [P, 52400], F32))
        w_query_ready = sem("w_query_ready")
        ident_ready = sem("ident_ready")

        top = [0]

        def carve(*shape):
            n = 1
            for s in shape:
                n *= s
            v = arena_t[:, top[0]:top[0] + n]
            top[0] += n
            assert top[0] <= 52400, top[0]
            if len(shape) == 2:
                v = v.rearrange("p (a b) -> p a b", a=shape[0])
            return v

        w_in_sb = carve(KD, W_IN)
        w_query_sb = arena_t[:, 0:KD * 2048].rearrange("p (a b) -> p a b", a=KD)
        subk_sb = arena_t[:, KD * 2048:KD * 2048 + 16 * P].rearrange("p (a b) -> p a b", a=16)
        shared_top = top[0]

        w_out_sb = carve(KD, D)
        overlay = top[0]
        bias_a_sb = carve(H, A_KEYS)
        bias_b_sb = carve(H, B_KEYS)
        end_overlay = top[0]
        top[0] = overlay
        ckT_sb = [carve(4, CA) for _ in range(2)]
        cv_sb = [carve(2, AW) for _ in range(2)]
        ckbT_sb = [carve(CB) for _ in range(2)]
        cvb_sb = [carve(P) for _ in range(2)]
        vnew_sb = [carve(AW + P) for _ in range(2)]
        qx_sb = [carve(640) for _ in range(2)]
        assert top[0] <= end_overlay, (top[0], end_overlay)
        top[0] = end_overlay
        qxb_sb = [carve(P) for _ in range(2)]
        bias_sa_sb = carve(CA + FR)
        bias_sb_sb = carve(CB + FR)
        k_win = carve(4, A_KEYS)
        v_win = carve(A_BLK, AW)
        kb_win = carve(B_KEYS)
        vb_win = carve(2, P)
        valid = carve(A_KEYS)
        x_sb = [carve(D) for _ in range(2)]
        xn = carve(D)
        xT = carve(KD, P)
        z = carve(13 * P)
        qT = carve(8, P)
        sc = [carve(A_KEYS) for _ in range(2)]
        pT = [carve(A_BLK, P) for _ in range(2)]
        g1_sb = carve(KD)
        g_ab_sb = carve(KD)
        sink_sb = carve(H + 1)
        ss = carve(4)
        rstd = carve(4)
        m_sb = carve(16)
        nm = carve(16)
        den = carve(16)
        rcp = carve(16)
        sd = carve(H)
        es = carve(H)
        m_s = [carve(2) for _ in range(2)]
        nm_s = [carve(2) for _ in range(2)]
        sd_s = [carve(1) for _ in range(2)]
        den_s = [carve(2) for _ in range(2)]
        es_s = [carve(1) for _ in range(2)]
        rcp_s = [carve(2) for _ in range(2)]

        const_in = sem("const_in")
        g1_in = sem("g1_in")
        w_in_in = [sem(f"w_in_in{c}") for c in range(5)]
        w_out_in = sem("w_out_in")
        x_in = [sem(f"x_in{p}") for p in range(2)]
        windows_clear = sem("windows_clear")
        pool_chain = sem("pool_chain")
        dve_chain = sem("dve_chain")
        ss_ready = sem("ss_ready")
        rms_ready = sem("rms_ready")
        xn_ready = sem("xn_ready")
        xT_psum = sem("xT_psum")
        xT_ready = sem("xT_ready")
        proj_psum = sem("proj_psum")
        z_ready = sem("z_ready")
        z_free = sem("z_free")
        kv_stored = sem("kv_stored")
        shifted = sem("shifted")
        qkT_psum = sem("qkT_psum")
        qkT_ready = sem("qkT_ready")
        s_psum = sem("s_psum")
        s_read = sem("s_read")
        nm_ready = sem("nm_ready")
        e_ready = sem("e_ready")
        pT_psum = sem("pT_psum")
        pT_ready = sem("pT_ready")
        o_psum = sem("o_psum")
        sd_ready = sem("sd_ready")
        es_ready = sem("es_ready")
        o_ready = sem("o_ready")
        sso_ready = sem("sso_ready")
        rmso_ready = sem("rmso_ready")
        on_ready = sem("on_ready")
        oT_psum = sem("oT_psum")
        oT_ready = sem("oT_ready")
        wo_psum = sem("wo_psum")
        h_ready = sem("h_ready")
        h_stored = sem("h_stored")
        new_kv_stored = sem("new_kv_stored")
        cache_in = [sem(f"cache_in{p}") for p in range(2)]
        qx_clear = sem("qx_clear")
        qx_ready = sem("qx_ready")
        ds_psum = sem("ds_psum")
        dnm_ready = sem("dnm_ready")
        de_ready = sem("de_ready")
        dp_ready = sem("dp_ready")
        dpT_psum = sem("dpT_psum")
        dpT_ready = sem("dpT_ready")
        doT_psum = sem("doT_psum")
        doT_ready = sem("doT_ready")
        do_psum = sem("do_psum")

        def gcol(g):
            return g.unsqueeze(2).broadcast_to([P, KD, P])

        with nc.Block() as block:

            @block.sync
            def _(sp):
                sp.dma_start(x_sb[0], x_prompt[0:P, :]).then_inc(x_in[0], 16)
                w_v = w_in.rearrange("(k p) n -> p k n", p=P)
                sp.dma_start(g1_sb, g1).then_inc(g1_in, 16)
                for c in range(5):
                    cols = slice(512 * c, min(512 * c + 512, W_IN))
                    sp.dma_start(w_in_sb[:, :, cols], w_v[:, :, cols]).then_inc(w_in_in[c], 16)
                sp.dma_start(x_sb[1], x_prompt[P:2 * P, :]).then_inc(x_in[1], 16)
                sp.dma_start(g_ab_sb, g_ab).then_inc(const_in, 16)
                sp.dma_start(sink_sb[:, 0:H], sinks[0:1, :].broadcast_to([P, H])).then_inc(const_in, 16)
                sp.dma_start(sink_sb[:, H:H + 1], sink_rows).then_inc(const_in, 16)
                sp.dma_start(bias_a_sb, bias_a).then_inc(const_in, 16)
                sp.dma_start(bias_b_sb, bias_b).then_inc(const_in, 16)
                sp.dma_start(bias_sa_sb, bias_sa).then_inc(const_in, 16)
                sp.dma_start(bias_sb_sb, bias_sb).then_inc(const_in, 16)
                sp.dma_start(w_out_sb, w_out.rearrange("(k p) n -> p k n", p=P)).then_inc(w_out_in, 16)

                def store_h(t, p):
                    sp.wait_ge(h_ready, 2 * t + 2 + CREDIT)
                    sp.dma_start(h_dram[bass.ds(t * P, P), :], x_sb[p]).then_inc(h_stored, 16)
                    sp.wait_ge(h_stored, 16 * t + 16)

                with sp.Fori(0, 2) as i:
                    for p in range(2):
                        sp.sem_inc(z_free, 1)
                        store_h(2 * i + p, p)
                        sp.dma_start(x_sb[p], x_prompt[bass.ds((2 * i + p + 2) * P, P), :])\
                          .then_inc(x_in[p], 16)
                for t in range(4, NT_PROMPT):
                    p = t % 2
                    rows = slice((t - 4) * P, (t - 3) * P)
                    sp.wait_ge(z_ready, 6 * t + 6)
                    sp.dma_start(ak_p[rows, :], z[:, AW:2 * AW]).then_inc(kv_stored, 16)
                    sp.dma_start(av_p[rows, :], v_win[:, A_BLK - 1, :]).then_inc(kv_stored, 16)
                    if t == NT_PROMPT - 1:
                        sp.dma_start(bk_p, z[:, 3 * AW:3 * AW + P]).then_inc(kv_stored, 16)
                        sp.dma_start(bv_p, vb_win[:, 1, :]).then_inc(kv_stored, 16)
                    sp.wait_ge(kv_stored, 32 * (t - 3) + (32 if t == NT_PROMPT - 1 else 0))
                    sp.sem_inc(z_free, 1)
                    store_h(t, p)
                    if t + 2 < NT_PROMPT:
                        sp.dma_start(x_sb[p], x_prompt[(t + 2) * P:(t + 3) * P, :]).then_inc(x_in[p], 16)
                    elif t + 2 == NT_PROMPT:
                        sp.dma_start(x_sb[p], x_sample).then_inc(x_in[p], 16)

                t = NT_PROMPT
                sp.wait_ge(z_ready, 6 * t + 6)
                sp.dma_start(ak_s, z[:, AW:2 * AW]).then_inc(new_kv_stored, 16)
                sp.dma_start(av_s, v_win[:, A_BLK - 1, :]).then_inc(new_kv_stored, 16)
                sp.dma_start(bk_s, z[:, 3 * AW:3 * AW + P]).then_inc(new_kv_stored, 16)
                sp.dma_start(bv_s, vb_win[:, 1, :]).then_inc(new_kv_stored, 16)
                sp.wait_ge(new_kv_stored, 64)

                def load_stream(b, p):
                    q = cache_in[p]
                    sp.dma_start(ckT_sb[p].rearrange("p a b -> p (a b)"),
                                 ckT[bass.ds(b * P, P), :]).then_inc(q, 16)
                    sp.dma_start(cv_sb[p], cv[bass.ds(b * CA, CA), :]
                                 .rearrange("(a p) c -> p a c", p=P)).then_inc(q, 16)
                    sp.dma_start(ckbT_sb[p], ckbT[bass.ds(b * P, P), :]).then_inc(q, 16)
                    sp.dma_start(cvb_sb[p], cvb[bass.ds(b * P, P), :]).then_inc(q, 16)
                    sp.dma_start(vnew_sb[p][0:FR, 0:AW], av_s[bass.ds(b * FR, FR), :]).then_inc(q, 16)
                    sp.dma_start(vnew_sb[p][0:FR, AW:AW + P], bv_s[bass.ds(b * FR, FR), :]).then_inc(q, 16)

                sp.wait_ge(nm_ready, 16 * NT_PROMPT)
                load_stream(0, 0)
                load_stream(1, 1)
                sp.dma_start(w_query_sb, w_query.rearrange("(k p) n -> p k n", p=P)).then_inc(w_query_ready, 16)
                sp.dma_start(subk_sb.rearrange("p a b -> p (a b)"), subk).then_inc(w_query_ready, 16)
                with sp.Fori(1, STREAMS // 2) as i:
                    for p in range(2):
                        sp.wait_ge(doT_psum, 2 * i + p - 1)
                        load_stream(2 * i + p, p)
                store_h(t, 0)

            @block.gpsimd
            def _(pool):
                for ahead in (oT_psum, z_free, o_psum, o_ready, h_ready, dpT_ready, doT_ready, ds_psum, sso_ready):
                    pool.sem_inc(ahead, CREDIT)
                ch = Chain(pool, pool_chain)
                ch.mark(pool.memset(ident, 0.0))
                ch.settle()
                pool.memset(eps, EPS).then_inc(ident_ready, 1)
                pool.affine_select(out=ident, in_=ident, compare_op=ALU.not_equal, fill=1.0, base=0,
                                   pattern=[[-1, P]], channel_multiplier=1).then_inc(ident_ready, 1)
                k2 = k_win.rearrange("p a b -> p (a b)")
                v2 = v_win.rearrange("p a b -> p (a b)")
                vb2 = vb_win.rearrange("p a b -> p (a b)")
                for w in (k2, v2, kb_win, vb2):
                    ch.mark(pool.memset(w, 0.0))
                ch.mark(pool.memset(valid, NEG))
                pool.wait_ge(const_in, 16 * 7)
                ch.settle()
                pool.memset(bias_a_sb[0:64, :, A_KEYS - 64:A_KEYS], NEG).then_inc(windows_clear, 1)
                pool.wait_ge(windows_clear, 1)
                pool.memset(bias_a_sb[64:P, :, 0:64], NEG).then_inc(windows_clear, 1)
                pool.wait_ge(windows_clear, 2)
                ch.restart()
                with pool.Fori(0, NT_PROMPT) as t:
                    pool.wait_ge(o_psum, 16 * t + CREDIT)
                    ch.pass_on()
                    for blk in range(A_BLK - 1):
                        a, b = blk * P, (blk + 1) * P
                        ch.mark(pool.tensor_copy(k_win[:, :, a:b], k_win[:, :, a + P:b + P]))
                        ch.mark(pool.tensor_copy(v_win[:, blk, :], v_win[:, blk + 1, :]))
                        ch.mark(pool.tensor_copy(valid[:, a:b], valid[:, a + P:b + P]))
                        if blk == 0:
                            ch.mark(pool.tensor_copy(kb_win[:, 0:P], kb_win[:, P:2 * P]))
                            ch.mark(pool.tensor_copy(vb_win[:, 0, :], vb_win[:, 1, :]))
                        ch.settle()
                    ch.restart()
                    pool.memset(valid[:, A_KEYS - P:A_KEYS], 0.0).then_inc(shifted, 1)
                pool.wait_ge(nm_ready, 16 * NT_PROMPT)
                for p in range(2):
                    pool.memset(qx_sb[p], 0.0).then_inc(qx_clear, 1)
                    pool.memset(qxb_sb[p], 0.0).then_inc(qx_clear, 1)

            @block.scalar
            def _(act):
                def project(t, u, p, prompt):
                    act.wait_ge(x_in[p], 16 * u + 16)
                    act.wait_ge(oT_psum, t + CREDIT)
                    act.activation(xn, x_sb[p], ACT.Square, accum_out=ss[:, 0:1]).then_inc(ss_ready, 1)
                    act.wait_ge(ss_ready, t + 1)
                    act.activation(rstd[:, 0:1], ss[:, 0:1], ACT.Sqrt, bias=eps, scale=1.0 / D)\
                       .then_inc(rms_ready, 1)
                    act.wait_ge(z_free, t + CREDIT)
                    act.wait_ge(proj_psum, 5 * t + 1)
                    act.copy(z[:, 0:AW], PS[:, 0, :]).then_inc(z_ready, 1)
                    act.wait_ge(proj_psum, 5 * t + 2)
                    act.copy(z[:, AW:2 * AW], PS[:, 1, :]).then_inc(z_ready, 1)
                    act.wait_ge(proj_psum, 5 * t + 3)
                    act.wait_ge(shifted, t + 1 if prompt else t)
                    act.copy(v_win[:, A_BLK - 1, :], PS[:, 2, :]).then_inc(z_ready, 1)
                    act.wait_ge(proj_psum, 5 * t + 4)
                    act.copy(z[:, 2 * AW:3 * AW], PS[:, 3, :]).then_inc(z_ready, 1)
                    act.wait_ge(proj_psum, 5 * t + 5)
                    act.copy(z[:, 3 * AW:3 * AW + P], PS[:, 4, 0:P]).then_inc(z_ready, 1)
                    act.copy(vb_win[:, 1, :], PS[:, 4, P:2 * P]).then_inc(z_ready, 1)
                    act.wait_ge(qkT_psum, 4 * t + 1)
                    act.mul(qT[:, 0:4, :].rearrange("p a b -> p (a b)"), PS[:, 5, :], SCALE).then_inc(qkT_ready, 1)
                    act.wait_ge(qkT_psum, 4 * t + 2)
                    act.copy(k_win[:, :, A_KEYS - P:A_KEYS],
                             PS[:, 6, :].rearrange("p (a b) -> p a b", a=4)).then_inc(qkT_ready, 1)
                    act.wait_ge(qkT_psum, 4 * t + 3)
                    act.mul(qT[:, 4:8, :].rearrange("p a b -> p (a b)"), PS[:, 7, :], SCALE).then_inc(qkT_ready, 1)
                    act.wait_ge(qkT_psum, 4 * t + 4)
                    act.copy(kb_win[:, P:2 * P], PS[:, 0, 0:P]).then_inc(qkT_ready, 1)

                def out_squares(t):
                    act.wait_ge(o_ready, 2 * t + 2 + CREDIT)
                    act.activation(sc[0][:, 0:AW], xn[:, 0:AW], ACT.Square,
                                   accum_out=ss[:, 1:2]).then_inc(sso_ready, 1)
                    act.activation(sc[1][:, 0:AW], xn[:, AW:D], ACT.Square,
                                   accum_out=ss[:, 2:3]).then_inc(sso_ready, 1)
                    act.wait_ge(sso_ready, 2 * t + 2 + CREDIT)
                    act.activation(rstd[:, 1:3], ss[:, 1:3], ACT.Sqrt, bias=eps, scale=1.0 / AW)\
                       .then_inc(rmso_ready, 1)

                def evacuate_pT(t, n):
                    w = A_BLK if n < H else 2
                    q = n % 2
                    act.wait_ge(pT_psum, 16 * t + n + 1)
                    if n >= 2:
                        act.wait_ge(o_psum, 16 * t + n - 1 + CREDIT)
                    dst = pT[q]
                    if w == A_BLK:
                        act.copy(dst[:, 4, :], PS[:, 6, 0:P]).then_inc(pT_ready, 1)
                    act.copy(dst[:, 0:min(w, 4), :].rearrange("p a b -> p (a b)"),
                             PS[:, 4 + q, 0:min(w, 4) * P]).then_inc(pT_ready, 1)

                act.wait_ge(ident_ready, 2)
                with act.Fori(0, NT_PROMPT // 2) as i:
                    for p in range(2):
                        t = 2 * i + p
                        project(t, i, p, True)
                        for n in range(16):
                            w = A_KEYS if n < H else B_KEYS
                            act.wait_ge(nm_ready, 16 * t + n + 1)
                            act.activation(sc[n % 2][:, 0:w], sc[n % 2][:, 0:w], ACT.Exp, bias=nm[:, n:n + 1],
                                           accum_out=den[:, n:n + 1]).then_inc(e_ready, 1)
                            if n:
                                evacuate_pT(t, n - 1)
                        evacuate_pT(t, 15)
                        act.wait_ge(sd_ready, t + 1)
                        act.activation(es, sd, ACT.Exp).then_inc(es_ready, 1)
                        out_squares(t)

                project(NT_PROMPT, NT_PROMPT // 2, 0, False)
                with act.Fori(0, STREAMS // 2) as i:
                    for p in range(2):
                        b = 2 * i + p
                        act.wait_ge(dnm_ready, 3 * b + 1)
                        act.activation(sc[0][:, 0:CA + FR], sc[0][:, 0:CA + FR], ACT.Exp, bias=nm_s[p][:, 0:1],
                                       accum_out=den_s[p][:, 0:1]).then_inc(de_ready, 1)
                        act.wait_ge(dnm_ready, 3 * b + 3)
                        act.activation(sc[1][:, 0:CB + FR], sc[1][:, 0:CB + FR], ACT.Exp, bias=nm_s[p][:, 1:2],
                                       accum_out=den_s[p][:, 1:2]).then_inc(de_ready, 1)
                        act.activation(es_s[p], sd_s[p], ACT.Exp).then_inc(de_ready, 1)
                        act.wait_ge(dpT_psum, b + 1)
                        act.copy(pT[p][:, 0:2, :].rearrange("p a b -> p (a b)"), PS[:, 4, 0:2 * P]).then_inc(dpT_ready, 1)
                        act.copy(pT[p][0:FR, 2, :], PS[0:FR, 4, 2 * P:3 * P]).then_inc(dpT_ready, 1)
                        act.copy(pT[p][:, 3, :], PS[:, 5, 0:P]).then_inc(dpT_ready, 1)
                        act.copy(pT[p][0:FR, 4, :], PS[0:FR, 5, P:2 * P]).then_inc(dpT_ready, 1)
                out_squares(NT_PROMPT)

            @block.vector
            def _(dve):
                ch = Chain(dve, dve_chain)

                def invert(r):
                    ch.mark(dve.reciprocal(r, r))
                    ch.settle()

                def norm(t, p):
                    dve.wait_ge(rms_ready, t + 1)
                    invert(rstd[:, 0:1])
                    dve.tensor_scalar(xn, x_sb[p], rstd[:, 0:1], None, ALU.mult).then_inc(xn_ready, 1)
                    dve.wait_ge(xT_psum, t + 1)
                    dve.tensor_tensor(xT, PS[:, 6:8, :].rearrange("p a (b c) -> p (a b) c", c=P), gcol(g1_sb),
                                      ALU.mult).then_inc(xT_ready, 1)

                def merge(t, p):
                    dve.wait_ge(rmso_ready, t + 1)
                    invert(rstd[:, 1:3])
                    dve.tensor_scalar(xn[:, 0:AW], xn[:, 0:AW], rstd[:, 1:2], None, ALU.mult).then_inc(on_ready, 1)
                    dve.tensor_scalar(xn[:, AW:D], xn[:, AW:D], rstd[:, 2:3], None, ALU.mult).then_inc(on_ready, 1)
                    dve.wait_ge(oT_psum, t + 1 + CREDIT)
                    dve.tensor_tensor(xT, PS[:, 0:2, :].rearrange("p a (b c) -> p (a b) c", c=P), gcol(g_ab_sb),
                                      ALU.mult).then_inc(oT_ready, 1)
                    for c in range(2):
                        dve.wait_ge(wo_psum, 2 * t + c + 1)
                        cols = slice(512 * c, 512 * c + 512)
                        dve.tensor_tensor(x_sb[p][:, cols], PS[:, 2 + c, :], x_sb[p][:, cols],
                                          ALU.add).then_inc(h_ready, 1)

                dve.wait_ge(g1_in, 16)
                with dve.Fori(0, NT_PROMPT // 2) as i:
                    for p in range(2):
                        t = 2 * i + p
                        norm(t, p)
                        dve.wait_ge(const_in, 16 * 7)
                        dve.wait_ge(windows_clear, 2)
                        dve.wait_ge(shifted, t + 1)
                        for n in range(16):
                            q = n % 2
                            h = n % H
                            group_a = n < H
                            dve.wait_ge(s_psum, 16 * t + n + 1)
                            if n >= 2:
                                dve.wait_ge(pT_psum, 16 * t + n - 1)
                            elif n == 0:
                                dve.wait_ge(sso_ready, 2 * t + CREDIT)
                            if group_a:
                                psum = PS[:, 2 * q:2 * q + 2, 0:A_KEYS // 2]
                                s3 = sc[q].rearrange("p (a b) -> p a b", a=2)
                                dve.tensor_tensor(s3, psum, valid.rearrange("p (a b) -> p a b", a=2), ALU.add)\
                                   .then_inc(s_read, 1)
                                s, bias, floor = sc[q], bias_a_sb[:, h, :], LOWEST
                            else:
                                s, bias, floor = sc[q][:, 0:B_KEYS], bias_b_sb[:, h, :], sink_sb[:, h:h + 1]
                                dve.tensor_tensor(s, PS[:, 2 * q, 0:B_KEYS], valid[:, A_KEYS - B_KEYS:A_KEYS],
                                                  ALU.add).then_inc(s_read, 1)
                            dve.wait_ge(s_read, 16 * t + n + 1)
                            ch.pass_on()
                            ch.mark(dve.tensor_tensor_reduce(s, s, bias, 1.0, floor, ALU.add, ALU.max, m_sb[:, n:n + 1]))
                            ch.settle()
                            dve.tensor_scalar(nm[:, n:n + 1], m_sb[:, n:n + 1], -1.0, None, ALU.mult)\
                               .then_inc(nm_ready, 1)
                        dve.wait_ge(nm_ready, 16 * t + 16)
                        dve.tensor_tensor(sd, nm[:, H:16], sink_sb[:, 0:H], ALU.add).then_inc(sd_ready, 1)
                        dve.wait_ge(es_ready, t + 1)
                        ch.mark(dve.tensor_tensor(den[:, H:16], den[:, H:16], es, ALU.add))
                        ch.settle()
                        ch.mark(dve.reciprocal(rcp, den))
                        ch.settle()
                        dve.wait_ge(o_psum, 16 * t + 16 + CREDIT)
                        for g in range(2):
                            dve.tensor_tensor(
                                xn[:, AW * g:AW * (g + 1)].rearrange("p (h d) -> p h d", h=H),
                                PS[:, 7 - g, :].rearrange("p (h d) -> p h d", h=H),
                                rcp[:, H * g:H * (g + 1)].unsqueeze(2).broadcast_to([P, H, HD]), ALU.mult)\
                               .then_inc(o_ready, 1)
                        merge(t, p)
                        ch.restart()

                norm(NT_PROMPT, 0)
                ch.restart()
                dve.wait_ge(qkT_ready, 4 * NT_PROMPT + 4)
                dve.wait_ge(qx_clear, 4)
                with dve.Fori(0, STREAMS // 2) as i:
                    for p in range(2):
                        b = 2 * i + p
                        fr = bass.ds(b * FR, FR)
                        dve.wait_ge(ds_psum, 2 * b + CREDIT)
                        qx = qx_sb[p].rearrange("p (j c) -> p j c", j=4)
                        dve.tensor_copy(qx[0:64, :, 0:FR], qT[0:64, 0:4, fr]).then_inc(qx_ready, 1)
                        dve.tensor_copy(qx[64:P, :, FR:2 * FR], qT[64:P, 0:4, fr]).then_inc(qx_ready, 1)
                        qxb = qxb_sb[p].rearrange("p (n g f) -> p n g f", n=2, g=4)
                        dve.tensor_copy(qxb[0:64, 0], qT[0:64, 4:8, fr]).then_inc(qx_ready, 1)
                        dve.tensor_copy(qxb[64:P, 1], qT[64:P, 4:8, fr]).then_inc(qx_ready, 1)
                        for g, (keys, bias, floor) in enumerate(((CA + FR, bias_sa_sb, LOWEST),
                                                                 (CB + FR, bias_sb_sb, sink_sb[:, H:H + 1]))):
                            dve.wait_ge(ds_psum, 2 * b + g + 1 + CREDIT)
                            ch.pass_on()
                            ch.mark(dve.tensor_tensor_reduce(sc[g][:, 0:keys], PS[:, 2 * g + p, 0:keys], bias,
                                                             1.0, floor, ALU.add, ALU.max, m_s[p][:, g:g + 1]))
                            ch.settle()
                            dve.tensor_scalar(nm_s[p][:, g:g + 1], m_s[p][:, g:g + 1], -1.0, None, ALU.mult)\
                               .then_inc(dnm_ready, 1)
                        dve.wait_ge(dnm_ready, 3 * b + 2)
                        dve.tensor_tensor(sd_s[p], nm_s[p][:, 1:2], sink_sb[:, H:H + 1], ALU.add)\
                           .then_inc(dnm_ready, 1)
                        dve.wait_ge(de_ready, 3 * b + 3)
                        ch.mark(dve.tensor_tensor(den_s[p][:, 1:2], den_s[p][:, 1:2], es_s[p], ALU.add))
                        ch.settle()
                        ch.mark(dve.reciprocal(rcp_s[p], den_s[p]))
                        ch.settle()
                        for g, keys in enumerate((CA + FR, CB + FR)):
                            dve.tensor_scalar(sc[g][:, 0:keys], sc[g][:, 0:keys], rcp_s[p][:, g:g + 1], None,
                                              ALU.mult).then_inc(dp_ready, 1)
                        dve.wait_ge(doT_psum, b + 1)
                        oa = PS[:, 6, 0:P].rearrange("p (j c) -> p j c", j=4)
                        ob = PS[:, 6, P:2 * P].rearrange("p (n g f) -> p n g f", n=2, g=4)
                        dve.tensor_copy(xT[0:64, 0:4, fr], oa[0:64, :, 0:FR]).then_inc(doT_ready, 1)
                        dve.tensor_copy(xT[64:P, 0:4, fr], oa[64:P, :, FR:2 * FR]).then_inc(doT_ready, 1)
                        dve.tensor_copy(xT[0:64, 4:8, fr], ob[0:64, 0]).then_inc(doT_ready, 1)
                        dve.tensor_copy(xT[64:P, 4:8, fr], ob[64:P, 1]).then_inc(doT_ready, 1)
                        ch.restart()
                dve.wait_ge(do_psum, 1)
                dve.tensor_copy(xn[:, 0:AW], PS[:, 0, :]).then_inc(o_ready, 1)
                dve.tensor_copy(xn[:, AW:D].rearrange("p (n g d) -> p g n d", n=2, g=4),
                                PS[:, 1, :].rearrange("p (g n d) -> p g n d", n=2, g=4)).then_inc(o_ready, 1)
                merge(NT_PROMPT, 0)

            @block.tensor
            def _(pe):
                def tr(bank, k, src):
                    return pe.transpose(PS[:, bank, k * P:(k + 1) * P], src, ident)

                def project(t):
                    pe.wait_ge(xn_ready, t + 1)
                    pe.wait_ge(o_ready, 2 * t + CREDIT)
                    for k in range(KD):
                        mm = tr(6 + k // 4, k % 4, xn[:, k * P:(k + 1) * P])
                    mm.then_inc(xT_psum, 1)
                    pe.wait_ge(xT_ready, t + 1)
                    pe.wait_ge(h_ready, 2 * t + CREDIT)
                    for c in range(5):
                        pe.wait_ge(w_in_in[c], 16)
                        w = min(512, W_IN - 512 * c)
                        for k in range(KD):
                            mm = pe.matmul(PS[:, c, 0:w], xT[:, k, :], w_in_sb[:, k, 512 * c:512 * c + w],
                                           start=(k == 0), stop=(k == KD - 1))
                        mm.then_inc(proj_psum, 1)
                    for g, (bank, z0, n) in enumerate(((5, 0, 4), (6, AW, 4), (7, 2 * AW, 4), (0, 3 * AW, 1))):
                        pe.wait_ge(z_ready, 6 * t + (1, 2, 4, 5)[g])
                        for k in range(n):
                            mm = tr(bank, k, z[:, z0 + k * P:z0 + (k + 1) * P])
                        mm.then_inc(qkT_psum, 1)

                def scores(t, n):
                    q = n % 2
                    if n >= 2:
                        pe.wait_ge(s_read, 16 * t + n - 1)
                    if n < H:
                        rows = slice(64 * (n % 2), 64 * (n % 2) + 64)
                        for c in range(2):
                            cols = slice(c * A_KEYS // 2, (c + 1) * A_KEYS // 2)
                            mm = pe.matmul(PS[:, 2 * q + c, 0:A_KEYS // 2], qT[rows, n // 2, :],
                                           k_win[rows, n // 2, cols], start=True, stop=True)
                    else:
                        kv, g = (n - H) // 4, (n - H) % 4
                        rows = slice(64 * kv, 64 * kv + 64)
                        mm = pe.matmul(PS[:, 2 * q, 0:B_KEYS], qT[rows, 4 + g, :], kb_win[rows, :],
                                       start=True, stop=True)
                    mm.then_inc(s_psum, 1)

                def turn(t, n):
                    q = n % 2
                    pe.wait_ge(e_ready, 16 * t + n + 1)
                    if n >= 2:
                        pe.wait_ge(pT_ready, PT0(t) + pT_count(n - 2))
                    for k in range(A_BLK if n < H else 2):
                        if k == 4 and n:
                            pe.wait_ge(pT_ready, PT0(t) + pT_count(n - 1) - 1)
                        mm = tr(4 + q if k < 4 else 6, k % 4, sc[q][:, k * P:(k + 1) * P])
                    mm.then_inc(pT_psum, 1)

                def PT0(t):
                    return 24 * t

                def pT_count(n):
                    return 2 * (n + 1) if n < H else 2 * H + n - H + 1

                def weigh(t, n):
                    pe.wait_ge(pT_ready, PT0(t) + pT_count(n))
                    if n < H:
                        for k in range(A_BLK):
                            mm = pe.matmul(PS[:, 7, n * HD:(n + 1) * HD], pT[n % 2][:, k, :],
                                           v_win[:, k, n * HD:(n + 1) * HD], start=(k == 0), stop=(k == A_BLK - 1))
                    else:
                        h = n - H
                        kv = h // 4
                        for k in range(2):
                            mm = pe.matmul(PS[:, 6, h * HD:(h + 1) * HD], pT[n % 2][:, k, :],
                                           vb_win[:, k, kv * HD:(kv + 1) * HD], start=(k == 0), stop=(k == 1))
                    mm.then_inc(o_psum, 1)

                def out_project(t):
                    pe.wait_ge(on_ready, 2 * t + 2)
                    for k in range(KD):
                        mm = tr(k // 4, k % 4, xn[:, k * P:(k + 1) * P])
                    mm.then_inc(oT_psum, 1)
                    pe.wait_ge(oT_ready, t + 1)
                    for c in range(2):
                        for k in range(KD):
                            mm = pe.matmul(PS[:, 2 + c, :], xT[:, k, :], w_out_sb[:, k, 512 * c:512 * c + 512],
                                           start=(k == 0), stop=(k == KD - 1))
                        mm.then_inc(wo_psum, 1)

                pe.wait_ge(ident_ready, 2)
                with pe.Fori(0, NT_PROMPT) as t:
                    project(t)
                    pe.wait_ge(w_out_in, 16)
                    pe.wait_ge(qkT_ready, 4 * t + 4)
                    scores(t, 0)
                    scores(t, 1)
                    for n in range(16):
                        turn(t, n)
                        if n + 2 < 16:
                            scores(t, n + 2)
                        if n:
                            weigh(t, n - 1)
                    weigh(t, 15)
                    out_project(t)

                project(NT_PROMPT)
                pe.wait_ge(qkT_ready, 4 * NT_PROMPT + 4)
                with pe.Fori(0, STREAMS // 2) as i:
                    for p in range(2):
                        b = 2 * i + p
                        pe.wait_ge(cache_in[p], 96 * i + 96)
                        pe.wait_ge(qx_ready, 4 * b + 4)
                        new = bass.ds(A_KEYS - P + b * FR, FR)
                        for keys, rhs in ((slice(0, CA), lambda j: ckT_sb[p][:, j, :]),
                                          (slice(CA, CA + FR), lambda j: k_win[:, j, new])):
                            for j in range(4):
                                mm = pe.matmul(PS[:, p, keys], qx_sb[p][:, j * P:(j + 1) * P], rhs(j),
                                               start=(j == 0), stop=(j == 3))
                        mm.then_inc(ds_psum, 1)
                        pe.matmul(PS[:, 2 + p, 0:CB], qxb_sb[p], ckbT_sb[p], start=True, stop=True)
                        pe.matmul(PS[:, 2 + p, CB:CB + FR], qxb_sb[p], kb_win[:, bass.ds(P + b * FR, FR)],
                                  start=True, stop=True).then_inc(ds_psum, 1)
                        pe.wait_ge(dp_ready, 2 * b + 2)
                        pe.wait_ge(dpT_ready, 4 * b + CREDIT)
                        tr(4, 0, sc[0][:, 0:P])
                        tr(4, 1, sc[0][:, P:CA])
                        pe.transpose(PS[0:FR, 4, 2 * P:3 * P], sc[0][:, CA:CA + FR], ident)
                        tr(5, 0, sc[1][:, 0:CB])
                        pe.transpose(PS[0:FR, 5, P:2 * P], sc[1][:, CB:CB + FR], ident).then_inc(dpT_psum, 1)
                        pe.wait_ge(dpT_ready, 4 * b + 4 + CREDIT)
                        pe.wait_ge(doT_ready, 4 * b + CREDIT)
                        for j in range(4):
                            out = PS[:, 6, 32 * j:32 * j + 32]
                            c = slice(32 * j, 32 * j + 32)
                            w = slice(j * P, (j + 1) * P)
                            for k in range(2):
                                pe.matmul(out, cv_sb[p][:, k, w], pT[p][:, k, c], start=(k == 0), stop=False)
                            pe.matmul(out, vnew_sb[p][0:FR, w], pT[p][0:FR, 2, c], start=False, stop=True)
                        pe.matmul(PS[:, 6, P:2 * P], cvb_sb[p], pT[p][:, 3, :], start=True, stop=False)
                        pe.matmul(PS[:, 6, P:2 * P], vnew_sb[p][0:FR, AW:AW + P], pT[p][0:FR, 4, :],
                                  start=False, stop=True).then_inc(doT_psum, 1)
                pe.wait_ge(doT_ready, 4 * STREAMS + CREDIT)
                for k in range(KD):
                    mm = tr(k // 4, k % 4, xT[:, k, :])
                mm.then_inc(do_psum, 1)
                out_project(NT_PROMPT)

        top[0] = shared_top
        uv = [carve(2 * D) for _ in range(RING)]
        x2 = [carve(D) for _ in range(2)]
        hb = [carve(D) for _ in range(2)]
        x2T = carve(KD, P)
        qT2 = carve(2 * QSP, P)
        s_sb = carve(16, P)
        s_left = carve(P)
        g2_bc = carve(D)
        gf_bc = carve(D)
        y_sb = carve(D)
        diag = carve(RING, P)
        rank = carve(CAND)
        onehot = carve(QSP * TOPK, CAND)
        sv = carve(16, TOPK)
        si_u = carve(16, TOPK).bitcast(U32)
        si = carve(16, TOPK)
        cand = carve(H, CAND)
        expert_of = carve(H, CAND)
        c_left = carve(CAND)
        fv = carve(H, TOPK)
        fi_u = carve(H, TOPK).bitcast(U32)
        fi = carve(H, TOPK)
        eidx = carve(SLOTS)
        expert_idx = [carve(SLOTS).bitcast(U32) for _ in range(2)]
        gate = [carve(SLOTS) for _ in range(2)]
        gden = carve(H)
        a_dot = [carve(GROUP) for _ in range(2)]
        a_gelu = [carve(GROUP) for _ in range(2)]
        wgt = [carve(GROUP) for _ in range(2)]
        ss2 = carve(2)
        rstd2 = carve(2)

        bc_in = sem("bc_in")
        h_in = [sem(f"h_in{p}") for p in range(2)]
        rank_ready = sem("rank_ready")
        chain_b = sem("chain_b")
        gather_chain = sem("gather_chain")
        ss2_ready = sem("ss2_ready")
        rms2_ready = sem("rms2_ready")
        x2_ready = sem("x2_ready")
        x2T_psum = sem("x2T_psum")
        x2T_ready = sem("x2T_ready")
        q_psum = sem("q_psum")
        q_ready = sem("q_ready")
        key_psum = sem("key_psum")
        key_ready = sem("key_ready")
        g_shift = sem("g_shift")
        g_exp = sem("g_exp")
        routed = sem("routed")
        uv_in = [sem(f"uv_in{s}") for s in range(RING)]
        dots_ready = sem("dots_ready")
        gelu_ready = sem("gelu_ready")
        wgt_ready = sem("wgt_ready")
        diag_ready = sem("diag_ready")
        slot_used = sem("slot_used")
        ssf_ready = sem("ssf_ready")
        rmsf_ready = sem("rmsf_ready")
        y_ready = sem("y_ready")
        y_stored = sem("y_stored")

        def pieces(run, route_part, finish):
            def tiles(t, u, p, more):
                for part in range(PARTS):
                    run(t, p, part)
                    if more:
                        route_part(t + 1, u + p, 1 - p, part)
                finish(t, p)
            return tiles

        with nc.Block() as block:

            @block.sync
            def _(sp):
                sp.dma_start(hb[0], h_dram[0:P, :]).then_inc(h_in[0], 16)
                sp.dma_start(g2_bc, g2[0:1, :].broadcast_to([P, D])).then_inc(bc_in, 16)
                sp.dma_start(gf_bc, gf[0:1, :].broadcast_to([P, D])).then_inc(bc_in, 16)
                sp.dma_start(hb[1], h_dram[P:2 * P, :]).then_inc(h_in[1], 16)

                def store(t, dst):
                    sp.wait_ge(y_ready, t + 1)
                    sp.dma_start(dst, y_sb).then_inc(y_stored, 16)

                with sp.Fori(0, 3) as i:
                    for p in range(2):
                        t = 2 * i + p
                        store(t, y_p[bass.ds(t * P, P), :])
                        sp.dma_start(hb[p], h_dram[bass.ds((t + 2) * P, P), :]).then_inc(h_in[p], 16)
                store(6, y_p[6 * P:7 * P, :])
                sp.dma_start(hb[0], h_dram[NT_PROMPT * P:NT * P, :]).then_inc(h_in[0], 16)
                store(7, y_p[7 * P:8 * P, :])
                store(NT_PROMPT, y_s)
                sp.wait_ge(y_stored, 16 * NT + 16 * CREDIT)

            @block.gpsimd
            def _(pool):
                pool.sem_inc(y_stored, 16 * CREDIT)
                pool.iota(rank, pattern=[[1, CAND]], base=0, channel_multiplier=0,
                          allow_small_or_imprecise_dtypes=True).then_inc(rank_ready, 1)

                ch = Chain(pool, gather_chain)

                def gathers(t, p):
                    pool.wait_ge(routed, t + 1)
                    ch.pass_on()
                    for s in range(SLOTS):
                        r = s % RING
                        if s >= RING or not isinstance(t, int) or t > 0:
                            pool.wait_ge(slot_used, t * SLOTS + s - RING + 1)
                            ch.pass_on()
                        pool.indirect_dma_start(
                            out=uv[r], out_offset=None, in_=experts,
                            in_offset=bass.IndirectOffsetOnAxis(ap=expert_idx[p][:, s:s + 1], axis=0))\
                            .then_inc(uv_in[r], 16)
                    ch.restart()

                gathers(0, 0)
                gathers(1, 1)
                with pool.Fori(1, 4) as i:
                    for p in range(2):
                        gathers(2 * i + p, p)
                gathers(NT_PROMPT, 0)

            @block.scalar
            def _(act):
                def run(t, p, part):
                    for g in range(TOPK // GROUP):
                        n = part * (TOPK // GROUP) + g
                        q = n % 2
                        grp = t * (SLOTS // GROUP) + n
                        act.wait_ge(dots_ready, grp * GROUP + GROUP)
                        act.activation(a_gelu[q], a_dot[q], ACT.Gelu).then_inc(gelu_ready, 1)
                        act.wait_ge(wgt_ready, grp + 1)
                        for k in range(GROUP):
                            s = n * GROUP + k
                            if s >= RING:
                                act.wait_ge(slot_used, t * SLOTS + s - RING + 1)
                            act.activation(diag[:, s % RING, :], ident, ACT.Copy,
                                           scale=wgt[q][:, k:k + 1]).then_inc(diag_ready, 1)

                def route_part(t, u, p, part):
                    if part == 0:
                        act.wait_ge(h_in[p], 16 * u + 16)
                        act.activation(x2[p], hb[p], ACT.Square, accum_out=ss2[:, 0:1]).then_inc(ss2_ready, 1)
                        act.wait_ge(ss2_ready, t + 1)
                        act.activation(rstd2[:, 0:1], ss2[:, 0:1], ACT.Sqrt, bias=eps, scale=1.0 / D)\
                           .then_inc(rms2_ready, 1)
                    if part < H // QSP:
                        k = part
                        act.wait_ge(q_psum, 4 * t + k + 1)
                        act.copy(qT2.rearrange("p a b -> p (a b)"), PS[:, 6, :]).then_inc(q_ready, 1)
                        act.wait_ge(key_psum, 4 * t + k + 1)
                        act.copy(s_sb[:, 4 * k:4 * k + 4, :].rearrange("p a b -> p (a b)"), PS[:, 7, :])\
                           .then_inc(key_ready, 1)
                    if part == PARTS - 1:
                        act.wait_ge(g_shift, t + 1)
                        act.activation(gate[p], gate[p], ACT.Exp).then_inc(g_exp, 1)

                def finish(t, p):
                    act.wait_ge(slot_used, (t + 1) * SLOTS)
                    act.wait_ge(y_stored, 16 * t + 16 * CREDIT)
                    act.activation(y_sb, PS[:, 2 * p:2 * p + 2, :].rearrange("p a b -> p (a b)"), ACT.Square,
                                   accum_out=ss2[:, 1:2]).then_inc(ssf_ready, 1)
                    act.wait_ge(ssf_ready, t + 1)
                    act.activation(rstd2[:, 1:2], ss2[:, 1:2], ACT.Sqrt, bias=eps, scale=1.0 / D)\
                       .then_inc(rmsf_ready, 1)

                tiles = pieces(run, route_part, finish)
                for part in range(PARTS):
                    route_part(0, 0, 0, part)
                with act.Fori(0, 4) as i:
                    for p in range(2):
                        tiles(2 * i + p, i, p, True)
                tiles(NT_PROMPT, NT_PROMPT // 2, 0, False)

            @block.vector
            def _(dve):
                ch = Chain(dve, chain_b)

                def run(t, p, part):
                    for g in range(TOPK // GROUP):
                        n = part * (TOPK // GROUP) + g
                        q = n % 2
                        for k in range(GROUP):
                            s = n * GROUP + k
                            r = s % RING
                            dve.wait_ge(uv_in[r], 16 * (t * (SLOTS // RING) + s // RING + 1))
                            dve.tensor_tensor_reduce(uv[r][:, 0:D], uv[r][:, 0:D], x2[p], 1.0, 0.0, ALU.mult,
                                                     ALU.add, a_dot[q][:, k:k + 1])\
                               .then_inc(dots_ready, 1)
                        grp = t * (SLOTS // GROUP) + n
                        dve.wait_ge(gelu_ready, grp + 1)
                        dve.tensor_tensor(wgt[q], a_gelu[q], gate[p][:, n * GROUP:(n + 1) * GROUP], ALU.mult)\
                           .then_inc(wgt_ready, 1)

                def top16(values, left, src, idx):
                    ch.mark(dve.max(values[:, 0:8], src))
                    ch.settle()
                    ch.mark(dve.match_replace(left, values[:, 0:8], src, LOWEST))
                    ch.mark(dve.max_index(idx[:, 0:8], values[:, 0:8], src))
                    ch.settle()
                    ch.mark(dve.max(values[:, 8:16], left))
                    ch.settle()
                    ch.mark(dve.max_index(idx[:, 8:16], values[:, 8:16], left))

                def route_part(t, u, p, part):
                    if part == 0:
                        dve.wait_ge(rms2_ready, t + 1)
                        ch.mark(dve.reciprocal(rstd2[:, 0:1], rstd2[:, 0:1]))
                        ch.settle()
                        dve.scalar_tensor_tensor(out=x2[p], in0=hb[p], scalar=rstd2[:, 0:1], in1=g2_bc,
                                                 op0=ALU.mult, op1=ALU.mult).then_inc(x2_ready, 1)
                        dve.wait_ge(x2T_psum, t + 1)
                        dve.tensor_copy(x2T.rearrange("p a b -> p (a b)"),
                                        PS[:, 4:6, :].rearrange("p a b -> p (a b)")).then_inc(x2T_ready, 1)
                    if 1 <= part <= H // QSP:
                        k = part - 1
                        dve.wait_ge(key_ready, 4 * t + k + 1)
                        ch.pass_on()
                        for l in range(4 * k, 4 * k + 4):
                            top16(sv[:, l, :], s_left, s_sb[:, l, :], si_u[:, l, :])
                    if part == 5:
                        ch.settle()
                        ch.mark(dve.tensor_copy(si, si_u))
                        ch.settle()
                        si4 = si.rearrange("p (h two) k -> p h two k", two=2)
                        sv4 = sv.rearrange("p (h two) k -> p h two k", two=2)
                        ch.mark(dve.tensor_scalar(si4[:, :, 0, :], si4[:, :, 0, :], float(NKEYS), None, ALU.mult))
                        ch.settle()
                        at = 0
                        for i, w in enumerate(ROWS):
                            if w == 1 and i and ROWS[i - 1] == 1:
                                continue
                            n = ROWS.count(1) if w == 1 else 1
                            for dst, v4 in ((cand, sv4), (expert_of, si4)):
                                if w == 1:
                                    a = v4[:, :, 0, i:i + n]
                                    b = v4[:, :, 1, 0:1].broadcast_to([P, H, n])
                                else:
                                    a = v4[:, :, 0, i:i + 1].broadcast_to([P, H, w])
                                    b = v4[:, :, 1, 0:w]
                                ch.mark(dve.tensor_tensor(dst[:, :, at:at + w * n], a, b, ALU.add))
                            at += w * n
                        assert at == CAND
                        ch.settle()
                    if part in (5, 6):
                        for h in range(4 * (part - 5), 4 * (part - 5) + 4):
                            top16(fv[:, h, :], c_left, cand[:, h, :], fi_u[:, h, :])
                        ch.settle()
                    if part in (6, 7):
                        if part == 6:
                            ch.mark(dve.tensor_copy(fi, fi_u))
                            ch.settle()
                        for k in range(2 * (part - 6), 2 * (part - 6) + 2):
                            hs = slice(QSP * k, QSP * (k + 1))
                            oh = onehot.rearrange("p (h k) c -> p h k c", h=QSP)
                            for h in range(QSP):
                                hh = QSP * k + h
                                ch.mark(dve.tensor_tensor(
                                    oh[:, h], rank.unsqueeze(1).broadcast_to([P, TOPK, CAND]),
                                    fi[:, hh, :].unsqueeze(2).broadcast_to([P, TOPK, CAND]), ALU.is_equal))
                            ch.settle()
                            for h in range(QSP):
                                hh = QSP * k + h
                                ch.mark(dve.tensor_tensor(
                                    oh[:, h], oh[:, h],
                                    expert_of[:, hh, :].unsqueeze(1).broadcast_to([P, TOPK, CAND]), ALU.mult))
                            ch.settle()
                            ch.mark(dve.tensor_reduce(eidx[:, QSP * TOPK * k:QSP * TOPK * (k + 1)], onehot, AX_X,
                                                      ALU.add))
                            ch.settle()
                    if part == 7:
                        ch.mark(dve.tensor_copy(expert_idx[p], eidx))
                        g3 = gate[p].rearrange("p (h k) -> p h k", h=H)
                        dve.tensor_tensor(g3, fv, fv[:, :, 0:1].broadcast_to([P, H, TOPK]), ALU.subtract)\
                           .then_inc(g_shift, 1)
                        dve.wait_ge(g_exp, t + 1)
                        ch.mark(dve.tensor_reduce(gden, g3, AX_X, ALU.add))
                        ch.settle()
                        ch.mark(dve.reciprocal(gden, gden))
                        ch.settle()
                        ch.mark(dve.tensor_tensor(g3, g3, gden.unsqueeze(2).broadcast_to([P, H, TOPK]), ALU.mult))
                        ch.settle()
                        dve.sem_inc(routed, 1)
                        ch.restart()

                def finish(t, p):
                    dve.wait_ge(rmsf_ready, t + 1)
                    ch.mark(dve.reciprocal(rstd2[:, 1:2], rstd2[:, 1:2]))
                    ch.restart()
                    dve.scalar_tensor_tensor(out=y_sb, in0=PS[:, 2 * p:2 * p + 2, :].rearrange("p a b -> p (a b)"),
                                             scalar=rstd2[:, 1:2], in1=gf_bc, op0=ALU.mult, op1=ALU.mult)\
                       .then_inc(y_ready, 1)

                dve.wait_ge(bc_in, 32)
                dve.wait_ge(rank_ready, 1)
                tiles = pieces(run, route_part, finish)
                for part in range(PARTS):
                    route_part(0, 0, 0, part)
                with dve.Fori(0, 4) as i:
                    for p in range(2):
                        tiles(2 * i + p, i, p, True)
                tiles(NT_PROMPT, NT_PROMPT // 2, 0, False)

            @block.tensor
            def _(pe):
                def run(t, p, part):
                    if part == 0:
                        for c in range(2):
                            pe.matmul(PS[:, 2 * p + c, :], ident, hb[p][:, 512 * c:512 * c + 512],
                                      start=True, stop=False)
                    for s in range(part * TOPK, (part + 1) * TOPK):
                        r = s % RING
                        pe.wait_ge(diag_ready, t * SLOTS + s + 1)
                        for c in range(2):
                            mm = pe.matmul(PS[:, 2 * p + c, :], diag[:, r, :],
                                           uv[r][:, D + 512 * c:D + 512 * c + 512], start=False,
                                           stop=(s == SLOTS - 1))
                        mm.then_inc(slot_used, 1)

                def route_part(t, u, p, part):
                    if part == 0:
                        pe.wait_ge(x2_ready, t + 1)
                        for k in range(KD):
                            mm = pe.transpose(PS[:, 4 + k // 4, (k % 4) * P:(k % 4 + 1) * P],
                                              x2[p][:, k * P:(k + 1) * P], ident)
                        mm.then_inc(x2T_psum, 1)
                        pe.wait_ge(x2T_ready, t + 1)
                    if part < H // QSP:
                        for l in range(4):
                            c = (4 * part + l) * P
                            for k in range(KD):
                                mm = pe.matmul(PS[:, 6, l * P:(l + 1) * P], w_query_sb[:, k, c:c + P], x2T[:, k, :],
                                               start=(k == 0), stop=(k == KD - 1))
                        mm.then_inc(q_psum, 1)
                        pe.wait_ge(q_ready, 4 * t + part + 1)
                        for l in range(4):
                            mm = pe.matmul(PS[:, 7, l * P:(l + 1) * P], qT2[:, l, :], subk_sb[:, 4 * part + l, :],
                                           start=True, stop=True)
                        mm.then_inc(key_psum, 1)

                def finish(t, p):
                    pass

                pe.wait_ge(w_query_ready, 32)
                tiles = pieces(run, route_part, finish)
                for part in range(PARTS):
                    route_part(0, 0, 0, part)
                with pe.Fori(0, 4) as i:
                    for p in range(2):
                        tiles(2 * i + p, i, p, True)
                tiles(NT_PROMPT, NT_PROMPT // 2, 0, False)


def kernel(x_prompt, x_sample, cache_a_k, cache_a_v, cache_b_k, cache_b_v, norm1_g, w_in, rel_bias, sinks,
           out_norm_a_g, out_norm_b_g, w_out, norm2_g, w_query, sub_keys, expert_u, expert_v, norm_f_g):
    import numpy as np
    import concourse.bacc as bacc
    from concourse import mybir as mb
    from concourse.bass_utils import run_bass_kernel_spmd as run

    rel = np.asarray(rel_bias)[0]
    dist = 512 + np.arange(128)[:, None] - np.arange(640)[None, :]
    bias_a = rel[:, np.clip(dist, -63, 256) + 63].transpose(1, 0, 2)
    dist_s = 256 + np.arange(16)[:, None] - np.arange(272)[None, :]
    bias_sa = rel[:, np.clip(dist_s, -63, 256) + 63].reshape(128, 272)
    slope = 2.0 ** -np.arange(1, 9, dtype=np.float32)
    q, c = np.arange(128)[:, None], np.arange(256)[None, :]
    outside = (c // 64 < q // 64) | (c // 64 > q // 64 + 2)
    bias_b = np.where(outside[:, None, :], np.float32(-1e30),
                      -slope[None, :, None] * np.abs(128 + q - c).astype(np.float32)[:, None, :]).astype(np.float32)
    kpos = np.abs(128 + np.arange(16)[:, None] - np.arange(144)[None, :]).astype(np.float32)
    bias_sb = (-slope[:, None, None] * kpos[None]).reshape(128, 144).astype(np.float32)
    w = np.asarray(w_in)[0]
    qb = w[:, 1536:2048].reshape(1024, 2, 4, 64).transpose(0, 2, 1, 3).reshape(1024, 512)
    w = np.concatenate([w[:, :1536], qb, w[:, 2048:]], axis=1)
    ck = np.asarray(cache_a_k)[0].transpose(0, 2, 3, 1).reshape(8, 4, 128, 256).transpose(0, 2, 1, 3)
    arrays = {
        "x_prompt": np.asarray(x_prompt).reshape(1024, 1024),
        "x_sample": np.asarray(x_sample).reshape(128, 1024),
        "ckT": ck.reshape(1024, 1024),
        "cv": np.asarray(cache_a_v)[0].reshape(8 * 256, 512),
        "ckbT": np.asarray(cache_b_k)[0].transpose(0, 2, 3, 1).reshape(8 * 128, 128),
        "cvb": np.asarray(cache_b_v)[0].reshape(8 * 128, 128),
        "g1": np.asarray(norm1_g)[0].reshape(8, 128).T,
        "w_in": w,
        "bias_a": bias_a, "bias_b": bias_b, "bias_sa": bias_sa, "bias_sb": bias_sb,
        "sinks": np.asarray(sinks),
        "sink_rows": np.repeat(np.asarray(sinks)[0], 16).reshape(128, 1),
        "g_ab": np.concatenate([np.asarray(out_norm_a_g)[0], np.asarray(out_norm_b_g)[0]]).reshape(8, 128).T,
        "w_out": np.asarray(w_out)[0],
        "g2": np.asarray(norm2_g),
        "w_query": np.asarray(w_query)[0],
        "subk": np.asarray(sub_keys)[0].transpose(3, 0, 1, 2).reshape(128, 2048),
        "experts": np.concatenate([np.asarray(expert_u)[0], np.asarray(expert_v)[0]], axis=1),
        "gf": np.asarray(norm_f_g).reshape(1, 1024),
    }
    nc = bacc.Bacc("TRN2", target_bir_lowering=False, num_devices=1)
    ins, sent = [], {}
    for name, a in arrays.items():
        a = np.ascontiguousarray(a)
        sent[f"in_{name}"] = a
        ins.append(nc.dram_tensor(f"in_{name}", a.shape, mb.dt.from_np(a.dtype), kind="ExternalInput").ap())
    shapes = [(1024, 1024), (128, 1024), (512, 512), (512, 512), (128, 128), (128, 128),
              (128, 512), (128, 512), (128, 128), (128, 128)]
    outs = [nc.dram_tensor(f"out_{i}", s, mb.dt.float32, kind="ExternalOutput").ap() for i, s in enumerate(shapes)]
    build(nc, ins, outs)
    r = run(nc, [sent], core_ids=[0]).results[0]
    final = [(1, 1024, 1024), (8, 16, 1024), (1, 1, 512, 8, 64), (1, 1, 512, 8, 64), (1, 1, 128, 2, 64),
             (1, 1, 128, 2, 64), (1, 8, 16, 8, 64), (1, 8, 16, 8, 64), (1, 8, 16, 2, 64), (1, 8, 16, 2, 64)]
    return tuple(np.asarray(r[f"out_{i}"]).reshape(s) for i, s in enumerate(final))
```

```python
import concourse.bass as bass
from concourse import mybir
from concourse.alu_op_type import AluOpType as ALU
from contextlib import ExitStack

F32 = mybir.dt.float32
U32 = mybir.dt.uint32
ACT = mybir.ActivationFunctionType
AX_X = mybir.AxisListType.X

P = 128
D = 1024
KD = D // P
HD = 64
H = 8
AW = H * HD
NT_PROMPT = 8
NT = 9
W_IN = 3 * AW + AW + 4 * HD
A_BLK = 5
A_KEYS = A_BLK * P
B_KEYS = 2 * P
STREAMS = 8
FR = 16
CA = 256
CB = 128
EPS = 1e-6
SCALE = HD ** -0.5
NEG = -1e30
LOWEST = -3.0e38
NKEYS = 128
TOPK = 16
ROWS = [TOPK // (i + 1) for i in range(TOPK)]
CAND = sum(ROWS)
SLOTS = H * TOPK
RING = 8
GROUP = 4
QSP = 2
PARTS = 16
PER_PART = SLOTS // PARTS
ROUTE_AT = {1: 0, 2: 1, 4: 2, 6: 3, 7: 4, 8: 5, 9: 6, 10: 7, 11: 8, 12: 9, 13: 10, 14: 11, 15: 12}
ROUTE_PIECES = range(13)
BEST_OF_SUMS = {5: range(0, 2), 6: range(2, 5), 7: range(5, 8)}
ARENA = 53000
Y_CREDIT = 2
CREDIT = 1


def item_parts(n):
    return 2 * (n + 1) if n < H else 2 * H + n - H + 1


TILE_PARTS = item_parts(15)


class Chain:

    def __init__(self, eng, sem):
        self.eng, self.sem, self.n = eng, sem, 0

    def restart(self):
        self.settle()
        self.eng.sem_clear(self.sem)
        self.n = 0

    def mark(self, ins):
        ins.then_inc(self.sem, 1)
        self.n += 1

    def pass_on(self):
        self.eng.sem_inc(self.sem, 1)
        self.n += 1
        self.settle()

    def settle(self):
        self.eng.wait_ge(self.sem, self.n)




def invert_rms(dve, ch, r, squares, tmp, width):
    v, q = tmp[:, 0, :], tmp[:, 1, :]
    ch.mark(dve.tensor_scalar(v, squares, 1.0 / width, EPS, ALU.mult, ALU.add))
    ch.mark(dve.reciprocal(r, r))
    ch.settle()
    ch.mark(dve.tensor_tensor(q, r, r, ALU.mult))
    ch.settle()
    ch.mark(dve.tensor_tensor(q, q, v, ALU.mult))
    ch.settle()
    ch.mark(dve.tensor_scalar(q, q, -0.5, 1.5, ALU.mult, ALU.add))
    ch.settle()
    ch.mark(dve.tensor_tensor(r, r, q, ALU.mult))
    ch.settle()


def build(nc, ins, outs):
    (x_prompt, x_sample, ckT, cv, ckbT, cvb, g1, w_in, bias_a, bias_b, bias_sa, bias_sb, sinks, sink_rows,
     g_ab, w_out, g2, w_query, subk, experts, gf) = ins
    (y_p, y_s, ak_p, av_p, bk_p, bv_p, ak_s, av_s, bk_s, bv_s) = outs
    h_dram = nc.dram_tensor("h_scratch", (NT * P, D), F32, kind="Internal").ap()

    ctx = ExitStack()
    with ctx:
        def sem(name):
            return ctx.enter_context(nc.semaphore(name))

        PS = ctx.enter_context(nc.psum_tensor("PS", [P, 8, 512], F32))
        ident_t = ctx.enter_context(nc.sbuf_tensor("ident", [P, P], F32))
        ident = ident_t[:, :]
        eps = ctx.enter_context(nc.sbuf_tensor("eps", [P, 1], F32))[:, :]
        arena_t = ctx.enter_context(nc.sbuf_tensor("arena", [P, ARENA], F32))
        w_query_ready = sem("w_query_ready")
        ident_ready = sem("ident_ready")

        top = [0]

        def carve(*shape):
            n = 1
            for s in shape:
                n *= s
            v = arena_t[:, top[0]:top[0] + n]
            top[0] += n
            assert top[0] <= ARENA, top[0]
            if len(shape) == 2:
                v = v.rearrange("p (a b) -> p a b", a=shape[0])
            return v

        w_in_sb = carve(KD, W_IN)
        w_query_sb = arena_t[:, 0:KD * 2048].rearrange("p (a b) -> p a b", a=KD)
        subk_sb = arena_t[:, KD * 2048:KD * 2048 + 16 * P].rearrange("p (a b) -> p a b", a=16)
        shared_top = top[0]

        w_out_sb = carve(KD, D)
        overlay = top[0]
        bias_a_sb = carve(H, A_KEYS)
        bias_b_sb = carve(H, B_KEYS)
        end_overlay = top[0]
        top[0] = overlay
        ckT_sb = [carve(4, CA) for _ in range(2)]
        cv_sb = [carve(2, AW) for _ in range(2)]
        ckbT_sb = [carve(CB) for _ in range(2)]
        cvb_sb = [carve(P) for _ in range(2)]
        vnew_sb = [carve(AW + P) for _ in range(2)]
        qx_sb = [carve(640) for _ in range(2)]
        assert top[0] <= end_overlay, (top[0], end_overlay)
        top[0] = end_overlay
        qxb_sb = [carve(P) for _ in range(2)]
        bias_sa_sb = carve(CA + FR)
        bias_sb_sb = carve(CB + FR)
        k_win = carve(4, A_KEYS)
        v_win = carve(A_BLK, AW)
        kb_win = carve(B_KEYS)
        vb_win = carve(2, P)
        valid = carve(A_KEYS)
        x_sb = [carve(D) for _ in range(2)]
        xn = carve(D)
        xT = carve(KD, P)
        o_sb = carve(D)
        oT = carve(KD, P)
        z = carve(W_IN)
        qT = carve(8, P)
        sc = [carve(A_KEYS) for _ in range(2)]
        pT = [carve(A_BLK, P) for _ in range(2)]
        g1_sb = carve(KD)
        g_ab_sb = carve(KD)
        sink_sb = carve(H + 1)
        ss = carve(4)
        rstd = carve(4)
        newton = carve(2, 2)
        m_sb = carve(16)
        nm = carve(16)
        den = carve(16)
        rcp = carve(16)
        sd = carve(H)
        es = carve(H)
        m_s = [carve(2) for _ in range(2)]
        nm_s = [carve(2) for _ in range(2)]
        sd_s = [carve(1) for _ in range(2)]
        den_s = [carve(2) for _ in range(2)]
        es_s = [carve(1) for _ in range(2)]
        rcp_s = [carve(2) for _ in range(2)]
        VA, KB = slice(2 * AW, 3 * AW), slice(4 * AW, 4 * AW + P)
        VB = slice(4 * AW + P, W_IN)

        S_BANK = (0, 1)
        S_OWN = 2
        PT_BANK = (3, 4)
        PT_OWN = 5
        OA_BANK = 6
        OB_BANK = 5
        UNIT = 7

        const_in = sem("const_in")
        g1_in = sem("g1_in")
        w_in_in = [sem(f"w_in_in{c}") for c in range(5)]
        w_out_in = sem("w_out_in")
        x_in = [sem(f"x_in{p}") for p in range(2)]
        windows_clear = sem("windows_clear")
        pool_chain = sem("pool_chain")
        dve_chain = sem("dve_chain")
        ss_ready = sem("ss_ready")
        rms_ready = sem("rms_ready")
        xn_ready = sem("xn_ready")
        xT_psum = sem("xT_psum")
        xT_ready = sem("xT_ready")
        proj_psum = sem("proj_psum")
        z_ready = sem("z_ready")
        z_free = sem("z_free")
        kv_stored = sem("kv_stored")
        shifted = sem("shifted")
        qkT_psum = sem("qkT_psum")
        qkT_ready = sem("qkT_ready")
        s_psum = sem("s_psum")
        s_read = sem("s_read")
        nm_ready = sem("nm_ready")
        e_ready = sem("e_ready")
        pT_psum = sem("pT_psum")
        pT_ready = sem("pT_ready")
        o_psum = sem("o_psum")
        sd_ready = sem("sd_ready")
        es_ready = sem("es_ready")
        o_ready = sem("o_ready")
        sso_ready = sem("sso_ready")
        rmso_ready = sem("rmso_ready")
        on_ready = sem("on_ready")
        oT_psum = sem("oT_psum")
        oT_ready = sem("oT_ready")
        wo_psum = sem("wo_psum")
        h_ready = sem("h_ready")
        h_stored = sem("h_stored")
        new_kv_stored = sem("new_kv_stored")
        cache_in = [sem(f"cache_in{p}") for p in range(2)]
        qx_clear = sem("qx_clear")
        qx_ready = sem("qx_ready")
        ds_psum = sem("ds_psum")
        dnm_ready = sem("dnm_ready")
        de_ready = sem("de_ready")
        dp_ready = sem("dp_ready")
        dpT_psum = sem("dpT_psum")
        dpT_ready = sem("dpT_ready")
        doT_psum = sem("doT_psum")
        doT_ready = sem("doT_ready")
        do_psum = sem("do_psum")

        NORM_AT = 3
        PIECE_AT = {5: 0, 7: 1, 9: 2, 11: 3, 12: 4, 13: 5, 14: 6}
        PIECES = range(7)

        def gcol(g, n):
            return g.unsqueeze(2).broadcast_to([P, n, P])

        with nc.Block() as block:

            @block.sync
            def _(sp):
                sp.dma_start(x_sb[0], x_prompt[0:P, :]).then_inc(x_in[0], 16)
                w_v = w_in.rearrange("(k p) n -> p k n", p=P)
                sp.dma_start(g1_sb, g1).then_inc(g1_in, 16)
                for c in range(5):
                    cols = slice(512 * c, min(512 * c + 512, W_IN))
                    sp.dma_start(w_in_sb[:, :, cols], w_v[:, :, cols]).then_inc(w_in_in[c], 16)
                sp.dma_start(x_sb[1], x_prompt[P:2 * P, :]).then_inc(x_in[1], 16)
                sp.dma_start(g_ab_sb, g_ab).then_inc(const_in, 16)
                sp.dma_start(sink_sb[:, 0:H], sinks[0:1, :].broadcast_to([P, H])).then_inc(const_in, 16)
                sp.dma_start(sink_sb[:, H:H + 1], sink_rows).then_inc(const_in, 16)
                sp.dma_start(bias_a_sb, bias_a).then_inc(const_in, 16)
                sp.dma_start(bias_b_sb, bias_b).then_inc(const_in, 16)
                sp.dma_start(bias_sa_sb, bias_sa).then_inc(const_in, 16)
                sp.dma_start(bias_sb_sb, bias_sb).then_inc(const_in, 16)
                sp.dma_start(w_out_sb, w_out.rearrange("(k p) n -> p k n", p=P)).then_inc(w_out_in, 16)

                def store_h(t, p):
                    sp.wait_ge(h_ready, 2 * t + 2 + CREDIT)
                    sp.dma_start(h_dram[bass.ds(t * P, P), :], x_sb[p]).then_inc(h_stored, 16)
                    sp.wait_ge(h_stored, 16 * t + 16)

                with sp.Fori(0, 2) as i:
                    for p in range(2):
                        sp.sem_inc(z_free, 1)
                        store_h(2 * i + p, p)
                        sp.dma_start(x_sb[p], x_prompt[bass.ds((2 * i + p + 2) * P, P), :])\
                          .then_inc(x_in[p], 16)
                for t in range(4, NT_PROMPT):
                    p = t % 2
                    rows = slice((t - 4) * P, (t - 3) * P)
                    sp.wait_ge(z_ready, 5 * t + 5)
                    sp.dma_start(ak_p[rows, :], z[:, AW:2 * AW]).then_inc(kv_stored, 16)
                    sp.dma_start(av_p[rows, :], z[:, VA]).then_inc(kv_stored, 16)
                    if t == NT_PROMPT - 1:
                        sp.dma_start(bk_p, z[:, KB]).then_inc(kv_stored, 16)
                        sp.dma_start(bv_p, z[:, VB]).then_inc(kv_stored, 16)
                    sp.wait_ge(kv_stored, 32 * (t - 3) + (32 if t == NT_PROMPT - 1 else 0))
                    sp.sem_inc(z_free, 1)
                    store_h(t, p)
                    if t + 2 < NT_PROMPT:
                        sp.dma_start(x_sb[p], x_prompt[(t + 2) * P:(t + 3) * P, :]).then_inc(x_in[p], 16)
                    elif t + 2 == NT_PROMPT:
                        sp.dma_start(x_sb[p], x_sample).then_inc(x_in[p], 16)
                    if t == NT_PROMPT - 1:
                        break

                t = NT_PROMPT
                sp.wait_ge(z_ready, 5 * t + 5)
                sp.dma_start(ak_s, z[:, AW:2 * AW]).then_inc(new_kv_stored, 16)
                sp.dma_start(av_s, z[:, VA]).then_inc(new_kv_stored, 16)
                sp.dma_start(bk_s, z[:, KB]).then_inc(new_kv_stored, 16)
                sp.dma_start(bv_s, z[:, VB]).then_inc(new_kv_stored, 16)
                sp.wait_ge(new_kv_stored, 64)

                def load_stream(b, p):
                    q = cache_in[p]
                    sp.dma_start(ckT_sb[p].rearrange("p a b -> p (a b)"),
                                 ckT[bass.ds(b * P, P), :]).then_inc(q, 16)
                    sp.dma_start(cv_sb[p], cv[bass.ds(b * CA, CA), :]
                                 .rearrange("(a p) c -> p a c", p=P)).then_inc(q, 16)
                    sp.dma_start(ckbT_sb[p], ckbT[bass.ds(b * P, P), :]).then_inc(q, 16)
                    sp.dma_start(cvb_sb[p], cvb[bass.ds(b * P, P), :]).then_inc(q, 16)
                    sp.dma_start(vnew_sb[p][0:FR, 0:AW], av_s[bass.ds(b * FR, FR), :]).then_inc(q, 16)
                    sp.dma_start(vnew_sb[p][0:FR, AW:AW + P], bv_s[bass.ds(b * FR, FR), :]).then_inc(q, 16)

                sp.wait_ge(nm_ready, 16 * NT_PROMPT)
                load_stream(0, 0)
                load_stream(1, 1)
                sp.dma_start(w_query_sb, w_query.rearrange("(k p) n -> p k n", p=P)).then_inc(w_query_ready, 16)
                sp.dma_start(subk_sb.rearrange("p a b -> p (a b)"), subk).then_inc(w_query_ready, 16)
                with sp.Fori(1, STREAMS // 2) as i:
                    for p in range(2):
                        sp.wait_ge(doT_psum, 2 * i + p - 1)
                        load_stream(2 * i + p, p)
                store_h(t, 0)

            @block.gpsimd
            def _(pool):
                for ahead in (z_free, o_psum, h_ready, dpT_ready, doT_ready, ds_psum, sso_ready, shifted):
                    pool.sem_inc(ahead, CREDIT)
                ch = Chain(pool, pool_chain)
                ch.mark(pool.memset(ident, 0.0))
                ch.settle()
                pool.memset(eps, EPS).then_inc(ident_ready, 1)
                pool.affine_select(out=ident, in_=ident, compare_op=ALU.not_equal, fill=1.0, base=0,
                                   pattern=[[-1, P]], channel_multiplier=1).then_inc(ident_ready, 1)
                k2 = k_win.rearrange("p a b -> p (a b)")
                v2 = v_win.rearrange("p a b -> p (a b)")
                vb2 = vb_win.rearrange("p a b -> p (a b)")
                for w in (k2, v2, kb_win, vb2):
                    ch.mark(pool.memset(w, 0.0))
                ch.mark(pool.memset(valid, NEG))
                ch.settle()

                def shift(t):
                    pool.wait_ge(o_psum, 16 * t + CREDIT)
                    ch.pass_on()
                    for blk in range(A_BLK - 1):
                        a, b = blk * P, (blk + 1) * P
                        ch.mark(pool.tensor_copy(k_win[:, :, a:b], k_win[:, :, a + P:b + P]))
                        ch.mark(pool.tensor_copy(v_win[:, blk, :], v_win[:, blk + 1, :]))
                        ch.mark(pool.tensor_copy(valid[:, a:b], valid[:, a + P:b + P]))
                        if blk == 0:
                            ch.mark(pool.tensor_copy(kb_win[:, 0:P], kb_win[:, P:2 * P]))
                            ch.mark(pool.tensor_copy(vb_win[:, 0, :], vb_win[:, 1, :]))
                        ch.settle()
                    ch.mark(pool.memset(valid[:, A_KEYS - P:A_KEYS], 0.0))
                    pool.wait_ge(z_ready, 5 * t + 5)
                    ch.pass_on()
                    ch.mark(pool.tensor_copy(v_win[:, A_BLK - 1, :], z[:, VA]))
                    ch.settle()
                    pool.tensor_copy(vb_win[:, 1, :], z[:, VB]).then_inc(shifted, 1)
                    ch.restart()

                shift(0)
                pool.wait_ge(const_in, 16 * 7)
                ch.settle()
                pool.memset(bias_a_sb[0:64, :, A_KEYS - 64:A_KEYS], NEG).then_inc(windows_clear, 1)
                pool.wait_ge(windows_clear, 1)
                pool.memset(bias_a_sb[64:P, :, 0:64], NEG).then_inc(windows_clear, 1)
                pool.wait_ge(windows_clear, 2)
                with pool.Fori(1, NT) as t:
                    shift(t)
                pool.wait_ge(nm_ready, 16 * NT_PROMPT)
                for p in range(2):
                    pool.memset(qx_sb[p], 0.0).then_inc(qx_clear, 1)
                    pool.memset(qxb_sb[p], 0.0).then_inc(qx_clear, 1)

            @block.scalar
            def _(act):
                def norm(t, u, p):
                    act.wait_ge(x_in[p], 16 * u + 16)
                    act.activation(xn, x_sb[p], ACT.Square, accum_out=ss[:, 0:1]).then_inc(ss_ready, 1)
                    act.wait_ge(ss_ready, t + 1)
                    act.activation(rstd[:, 0:1], ss[:, 0:1], ACT.Sqrt, bias=eps, scale=1.0 / D)\
                       .then_inc(rms_ready, 1)

                def piece(t, k):
                    if k < 2:
                        return
                    c = k - 2
                    if c == 0:
                        act.wait_ge(z_free, t + CREDIT)
                        act.wait_ge(shifted, t + CREDIT)
                    act.wait_ge(proj_psum, 5 * t + c + 1)
                    w = min(512, W_IN - 512 * c)
                    act.copy(z[:, 512 * c:512 * c + w], PS[:, UNIT, 0:w]).then_inc(z_ready, 1)

                def queries_T(t):
                    for n, (bank, half) in enumerate(((0, 0), (2, 4))):
                        act.wait_ge(qkT_psum, 4 * t + n + 1)
                        act.mul(qT[:, half:half + 4, :].rearrange("p a b -> p (a b)"), PS[:, bank, :], SCALE)\
                           .then_inc(qkT_ready, 1)

                def keys_T(t):
                    act.wait_ge(qkT_psum, 4 * t + 3)
                    act.wait_ge(shifted, t + 1 + CREDIT)
                    act.copy(k_win[:, :, A_KEYS - P:A_KEYS],
                             PS[:, 1, :].rearrange("p (a b) -> p a b", a=4)).then_inc(qkT_ready, 1)
                    act.wait_ge(qkT_psum, 4 * t + 4)
                    act.copy(kb_win[:, P:2 * P], PS[:, 3, 0:P]).then_inc(qkT_ready, 1)

                def out_squares(t):
                    act.wait_ge(o_ready, 2 * t + 2)
                    act.activation(sc[0][:, 0:AW], o_sb[:, 0:AW], ACT.Square,
                                   accum_out=ss[:, 1:2]).then_inc(sso_ready, 1)
                    act.activation(sc[1][:, 0:AW], o_sb[:, AW:D], ACT.Square,
                                   accum_out=ss[:, 2:3]).then_inc(sso_ready, 1)
                    act.wait_ge(sso_ready, 2 * t + 2 + CREDIT)
                    act.activation(rstd[:, 1:3], ss[:, 1:3], ACT.Sqrt, bias=eps, scale=1.0 / AW)\
                       .then_inc(rmso_ready, 1)

                def evacuate_pT(t, n):
                    q = n % 2
                    act.wait_ge(pT_psum, 16 * t + n + 1)
                    if n >= 2:
                        act.wait_ge(o_psum, 16 * t + n - 1 + CREDIT)
                    w = 2
                    if n < H:
                        act.copy(pT[q][:, 4, :], PS[:, PT_OWN, 0:P]).then_inc(pT_ready, 1)
                        w = 4
                    act.copy(pT[q][:, 0:w, :].rearrange("p a b -> p (a b)"),
                             PS[:, PT_BANK[q], 0:w * P]).then_inc(pT_ready, 1)

                act.wait_ge(ident_ready, 2)
                norm(0, 0, 0)
                for k in PIECES:
                    piece(0, k)
                queries_T(0)
                keys_T(0)
                with act.Fori(0, NT_PROMPT // 2) as i:
                    for p in range(2):
                        t = 2 * i + p
                        for n in range(16):
                            w = A_KEYS if n < H else B_KEYS
                            act.wait_ge(nm_ready, 16 * t + n + 1)
                            act.activation(sc[n % 2][:, 0:w], sc[n % 2][:, 0:w], ACT.Exp, bias=nm[:, n:n + 1],
                                           accum_out=den[:, n:n + 1]).then_inc(e_ready, 1)
                            if n:
                                evacuate_pT(t, n - 1)
                            if n == NORM_AT:
                                norm(t + 1, i + p, 1 - p)
                            if n - 1 in PIECE_AT:
                                piece(t + 1, PIECE_AT[n - 1])
                        evacuate_pT(t, 15)
                        act.wait_ge(sd_ready, t + 1)
                        act.activation(es, sd, ACT.Exp).then_inc(es_ready, 1)
                        queries_T(t + 1)
                        out_squares(t)
                        keys_T(t + 1)

                def stream(b, p):
                    s = sc[p]
                    act.wait_ge(dnm_ready, 3 * b + 1)
                    act.activation(s[:, 0:CA + FR], s[:, 0:CA + FR], ACT.Exp, bias=nm_s[p][:, 0:1],
                                   accum_out=den_s[p][:, 0:1]).then_inc(de_ready, 1)
                    act.wait_ge(dnm_ready, 3 * b + 3)
                    sb = s[:, CA + FR:CA + FR + CB + FR]
                    act.activation(sb, sb, ACT.Exp, bias=nm_s[p][:, 1:2],
                                   accum_out=den_s[p][:, 1:2]).then_inc(de_ready, 1)
                    act.activation(es_s[p], sd_s[p], ACT.Exp).then_inc(de_ready, 1)
                    act.wait_ge(dpT_psum, b + 1)
                    act.copy(pT[p][:, 0:2, :].rearrange("p a b -> p (a b)"), PS[:, 4, 0:2 * P]).then_inc(dpT_ready, 1)
                    act.copy(pT[p][0:FR, 2, :], PS[0:FR, 4, 2 * P:3 * P]).then_inc(dpT_ready, 1)
                    act.copy(pT[p][:, 3, :], PS[:, 5, 0:P]).then_inc(dpT_ready, 1)
                    act.copy(pT[p][0:FR, 4, :], PS[0:FR, 5, P:2 * P]).then_inc(dpT_ready, 1)

                with act.Fori(0, STREAMS // 2) as i:
                    for p in range(2):
                        stream(2 * i + p, p)
                out_squares(NT_PROMPT)

            @block.vector
            def _(dve):
                ch = Chain(dve, dve_chain)

                def norm(t, p):
                    dve.wait_ge(rms_ready, t + 1)
                    invert_rms(dve, ch, rstd[:, 0:1], ss[:, 0:1], newton[:, :, 0:1], D)
                    dve.tensor_scalar(xn, x_sb[p], rstd[:, 0:1], None, ALU.mult).then_inc(xn_ready, 1)

                def piece(t, k):
                    if k < 2:
                        dve.wait_ge(xT_psum, 2 * t + k + 1)
                        dve.tensor_tensor(xT[:, 4 * k:4 * k + 4, :], PS[:, UNIT, :].rearrange("p (b c) -> p b c", c=P),
                                          gcol(g1_sb[:, 4 * k:4 * k + 4], 4), ALU.mult).then_inc(xT_ready, 1)

                def merge(t, p):
                    dve.wait_ge(rmso_ready, t + 1)
                    invert_rms(dve, ch, rstd[:, 1:3], ss[:, 1:3], newton, AW)
                    dve.tensor_scalar(o_sb[:, 0:AW], o_sb[:, 0:AW], rstd[:, 1:2], None, ALU.mult).then_inc(on_ready, 1)
                    dve.tensor_scalar(o_sb[:, AW:D], o_sb[:, AW:D], rstd[:, 2:3], None, ALU.mult).then_inc(on_ready, 1)
                    dve.wait_ge(oT_psum, t + 1)
                    dve.tensor_tensor(oT, PS[:, 4:6, :].rearrange("p a (b c) -> p (a b) c", c=P), gcol(g_ab_sb, KD),
                                      ALU.mult).then_inc(oT_ready, 1)
                    for c in range(2):
                        dve.wait_ge(wo_psum, 2 * t + c + 1)
                        cols = slice(512 * c, 512 * c + 512)
                        dve.tensor_tensor(x_sb[p][:, cols], PS[:, 6 + c, :], x_sb[p][:, cols],
                                          ALU.add).then_inc(h_ready, 1)

                def item(t, n):
                    q = n % 2
                    h = n % H
                    dve.wait_ge(s_psum, 16 * t + n + 1)
                    if n >= 2:
                        dve.wait_ge(pT_psum, 16 * t + n - 1)
                    elif n == 0:
                        dve.wait_ge(sso_ready, 2 * t + CREDIT)
                    if n < H:
                        dve.tensor_copy(sc[q][:, 4 * P:A_KEYS], PS[:, S_OWN, 0:P]).then_inc(s_read, 1)
                        dve.tensor_tensor(sc[q][:, 0:4 * P], PS[:, S_BANK[q], :], valid[:, 0:4 * P], ALU.add)\
                           .then_inc(s_read, 1)
                        s, bias, floor = sc[q], bias_a_sb[:, h, :], LOWEST
                    else:
                        s, bias, floor = sc[q][:, 0:B_KEYS], bias_b_sb[:, h, :], sink_sb[:, h:h + 1]
                        dve.tensor_tensor(s, PS[:, S_BANK[q], 0:B_KEYS], valid[:, A_KEYS - B_KEYS:A_KEYS],
                                          ALU.add).then_inc(s_read, 1)
                    dve.wait_ge(s_read, TILE_PARTS * t + item_parts(n))
                    ch.pass_on()
                    ch.mark(dve.tensor_tensor_reduce(s, s, bias, 1.0, floor, ALU.add, ALU.max, m_sb[:, n:n + 1]))
                    ch.settle()
                    dve.tensor_scalar(nm[:, n:n + 1], m_sb[:, n:n + 1], -1.0, None, ALU.mult)\
                       .then_inc(nm_ready, 1)

                dve.wait_ge(g1_in, 16)
                norm(0, 0)
                for k in PIECES:
                    piece(0, k)
                ch.restart()
                dve.wait_ge(const_in, 16 * 7)
                dve.wait_ge(windows_clear, 2)
                with dve.Fori(0, NT_PROMPT // 2) as i:
                    for p in range(2):
                        t = 2 * i + p
                        dve.wait_ge(shifted, t + 1 + CREDIT)
                        for n in range(16):
                            item(t, n)
                            if n == NORM_AT:
                                norm(t + 1, 1 - p)
                            if n - 1 in PIECE_AT:
                                piece(t + 1, PIECE_AT[n - 1])
                        dve.wait_ge(nm_ready, 16 * t + 16)
                        dve.tensor_tensor(sd, nm[:, H:16], sink_sb[:, 0:H], ALU.add).then_inc(sd_ready, 1)
                        dve.wait_ge(es_ready, t + 1)
                        ch.mark(dve.tensor_tensor(den[:, H:16], den[:, H:16], es, ALU.add))
                        ch.settle()
                        ch.mark(dve.reciprocal(rcp, den))
                        ch.settle()
                        dve.wait_ge(o_psum, 16 * t + 16 + CREDIT)
                        for g, bank in enumerate((OA_BANK, OB_BANK)):
                            dve.tensor_tensor(
                                o_sb[:, AW * g:AW * (g + 1)].rearrange("p (h d) -> p h d", h=H),
                                PS[:, bank, :].rearrange("p (h d) -> p h d", h=H),
                                rcp[:, H * g:H * (g + 1)].unsqueeze(2).broadcast_to([P, H, HD]), ALU.mult)\
                               .then_inc(o_ready, 1)
                        merge(t, p)
                        ch.restart()

                def expand(b, p):
                    fr = bass.ds(b * FR, FR)
                    qx = qx_sb[p].rearrange("p (j c) -> p j c", j=4)
                    dve.tensor_copy(qx[0:64, :, 0:FR], qT[0:64, 0:4, fr]).then_inc(qx_ready, 1)
                    dve.tensor_copy(qx[64:P, :, FR:2 * FR], qT[64:P, 0:4, fr]).then_inc(qx_ready, 1)
                    qxb = qxb_sb[p].rearrange("p (n g f) -> p n g f", n=2, g=4)
                    dve.tensor_copy(qxb[0:64, 0], qT[0:64, 4:8, fr]).then_inc(qx_ready, 1)
                    dve.tensor_copy(qxb[64:P, 1], qT[64:P, 4:8, fr]).then_inc(qx_ready, 1)

                def collect(b):
                    fr = bass.ds(b * FR, FR)
                    dve.wait_ge(doT_psum, b + 1)
                    oa = PS[:, 6, 0:P].rearrange("p (j c) -> p j c", j=4)
                    ob = PS[:, 6, P:2 * P].rearrange("p (n g f) -> p n g f", n=2, g=4)
                    dve.tensor_copy(xT[0:64, 0:4, fr], oa[0:64, :, 0:FR]).then_inc(doT_ready, 1)
                    dve.tensor_copy(xT[64:P, 0:4, fr], oa[64:P, :, FR:2 * FR]).then_inc(doT_ready, 1)
                    dve.tensor_copy(xT[0:64, 4:8, fr], ob[0:64, 0]).then_inc(doT_ready, 1)
                    dve.tensor_copy(xT[64:P, 4:8, fr], ob[64:P, 1]).then_inc(doT_ready, 1)

                def stream(b, p, first=False, last=False):
                    cols = (slice(0, CA + FR), slice(CA + FR, CA + FR + CB + FR))
                    for g, (bias, floor) in enumerate(((bias_sa_sb, LOWEST), (bias_sb_sb, sink_sb[:, H:H + 1]))):
                        dve.wait_ge(ds_psum, 2 * b + g + 1 + CREDIT)
                        ch.pass_on()
                        keys = cols[g].stop - cols[g].start
                        ch.mark(dve.tensor_tensor_reduce(sc[p][:, cols[g]], PS[:, 2 * g + p, 0:keys], bias,
                                                         1.0, floor, ALU.add, ALU.max, m_s[p][:, g:g + 1]))
                        ch.settle()
                        dve.tensor_scalar(nm_s[p][:, g:g + 1], m_s[p][:, g:g + 1], -1.0, None, ALU.mult)\
                           .then_inc(dnm_ready, 1)
                    dve.wait_ge(dnm_ready, 3 * b + 2)
                    dve.tensor_tensor(sd_s[p], nm_s[p][:, 1:2], sink_sb[:, H:H + 1], ALU.add)\
                       .then_inc(dnm_ready, 1)
                    if not last:
                        expand(b + 1, 1 - p)
                    if not first:
                        collect(b - 1)
                    dve.wait_ge(de_ready, 3 * b + 3)
                    ch.mark(dve.tensor_tensor(den_s[p][:, 1:2], den_s[p][:, 1:2], es_s[p], ALU.add))
                    ch.settle()
                    ch.mark(dve.reciprocal(rcp_s[p], den_s[p]))
                    ch.settle()
                    for g in range(2):
                        dve.tensor_scalar(sc[p][:, cols[g]], sc[p][:, cols[g]], rcp_s[p][:, g:g + 1], None,
                                          ALU.mult).then_inc(dp_ready, 1)
                    ch.restart()

                dve.wait_ge(qkT_ready, 4 * NT_PROMPT + 4)
                dve.wait_ge(qx_clear, 4)
                expand(0, 0)
                stream(0, 0, first=True)
                stream(1, 1)
                with dve.Fori(1, STREAMS // 2 - 1) as i:
                    for p in range(2):
                        stream(2 * i + p, p)
                stream(6, 0)
                stream(7, 1, last=True)
                collect(7)
                dve.wait_ge(do_psum, 1)
                dve.tensor_copy(o_sb[:, 0:AW], PS[:, 0, :]).then_inc(o_ready, 1)
                dve.tensor_copy(o_sb[:, AW:D].rearrange("p (n g d) -> p g n d", n=2, g=4),
                                PS[:, 1, :].rearrange("p (g n d) -> p g n d", n=2, g=4)).then_inc(o_ready, 1)
                merge(NT_PROMPT, 0)

            @block.tensor
            def _(pe):
                def tr(bank, k, src):
                    return pe.transpose(PS[:, bank, k * P:(k + 1) * P], src, ident)

                def piece(t, k):
                    if k < 2:
                        if k == 0:
                            pe.wait_ge(xn_ready, t + 1)
                        else:
                            pe.wait_ge(xT_ready, 2 * t + 1)
                        for j in range(4):
                            mm = tr(UNIT, j, xn[:, (4 * k + j) * P:(4 * k + j + 1) * P])
                        mm.then_inc(xT_psum, 1)
                        return
                    c = k - 2
                    pe.wait_ge(w_in_in[c], 16)
                    if c == 0:
                        pe.wait_ge(xT_ready, 2 * t + 2)
                    else:
                        pe.wait_ge(z_ready, 5 * t + c)
                    w = min(512, W_IN - 512 * c)
                    for j in range(KD):
                        mm = pe.matmul(PS[:, UNIT, 0:w], xT[:, j, :], w_in_sb[:, j, 512 * c:512 * c + w],
                                       start=(j == 0), stop=(j == KD - 1))
                    mm.then_inc(proj_psum, 1)

                def turn_qk(t):
                    pe.wait_ge(z_ready, 5 * t + 5)
                    for bank, z0, n in ((0, 0, 4), (2, 3 * AW, 4), (1, AW, 4), (3, 4 * AW, 1)):
                        for k in range(n):
                            mm = tr(bank, k, z[:, z0 + k * P:z0 + (k + 1) * P])
                        mm.then_inc(qkT_psum, 1)

                def scores(t, n):
                    q = n % 2
                    if n >= 2:
                        pe.wait_ge(s_read, TILE_PARTS * t + item_parts(n - 2))
                    if n < H:
                        rows = slice(64 * (n % 2), 64 * (n % 2) + 64)
                        mm = pe.matmul(PS[:, S_BANK[q], :], qT[rows, n // 2, :], k_win[rows, n // 2, 0:4 * P],
                                       start=True, stop=True)
                        if n:
                            pe.wait_ge(s_read, TILE_PARTS * t + item_parts(n - 1) - 1)
                        mm = pe.matmul(PS[:, S_OWN, 0:P], qT[rows, n // 2, :], k_win[rows, n // 2, 4 * P:A_KEYS],
                                       start=True, stop=True)
                    else:
                        kv, g = (n - H) // 4, (n - H) % 4
                        rows = slice(64 * kv, 64 * kv + 64)
                        mm = pe.matmul(PS[:, S_BANK[q], 0:B_KEYS], qT[rows, 4 + g, :], kb_win[rows, :],
                                       start=True, stop=True)
                    mm.then_inc(s_psum, 1)

                def turn(t, n):
                    q = n % 2
                    pe.wait_ge(e_ready, 16 * t + n + 1)
                    if n >= 2:
                        pe.wait_ge(pT_ready, TILE_PARTS * t + item_parts(n - 2))
                    for k in range(A_BLK if n < H else 2):
                        if k == 4 and n:
                            pe.wait_ge(pT_ready, TILE_PARTS * t + item_parts(n - 1) - 1)
                        mm = tr(PT_BANK[q] if k < 4 else PT_OWN, k % 4, sc[q][:, k * P:(k + 1) * P])
                    mm.then_inc(pT_psum, 1)

                def weigh(t, n):
                    pe.wait_ge(pT_ready, TILE_PARTS * t + item_parts(n))
                    if n < H:
                        for k in range(A_BLK):
                            mm = pe.matmul(PS[:, OA_BANK, n * HD:(n + 1) * HD], pT[n % 2][:, k, :],
                                           v_win[:, k, n * HD:(n + 1) * HD], start=(k == 0), stop=(k == A_BLK - 1))
                    else:
                        h = n - H
                        kv = h // 4
                        for k in range(2):
                            mm = pe.matmul(PS[:, OB_BANK, h * HD:(h + 1) * HD], pT[n % 2][:, k, :],
                                           vb_win[:, k, kv * HD:(kv + 1) * HD], start=(k == 0), stop=(k == 1))
                    mm.then_inc(o_psum, 1)

                def out_project(t):
                    pe.wait_ge(on_ready, 2 * t + 2)
                    for k in range(KD):
                        mm = tr(4 + k // 4, k % 4, o_sb[:, k * P:(k + 1) * P])
                    mm.then_inc(oT_psum, 1)
                    pe.wait_ge(oT_ready, t + 1)
                    for c in range(2):
                        for k in range(KD):
                            mm = pe.matmul(PS[:, 6 + c, :], oT[:, k, :], w_out_sb[:, k, 512 * c:512 * c + 512],
                                           start=(k == 0), stop=(k == KD - 1))
                        mm.then_inc(wo_psum, 1)

                pe.wait_ge(ident_ready, 2)
                for k in PIECES:
                    piece(0, k)
                turn_qk(0)
                with pe.Fori(0, NT_PROMPT) as t:
                    pe.wait_ge(qkT_ready, 4 * t + 4)
                    scores(t, 0)
                    scores(t, 1)
                    pe.wait_ge(shifted, t + 1 + CREDIT)
                    pe.wait_ge(h_ready, 2 * t + CREDIT)
                    for n in range(16):
                        turn(t, n)
                        if n + 2 < 16:
                            scores(t, n + 2)
                        if n:
                            weigh(t, n - 1)
                        if n in PIECE_AT:
                            piece(t + 1, PIECE_AT[n])
                    weigh(t, 15)
                    turn_qk(t + 1)
                    pe.wait_ge(w_out_in, 16)
                    out_project(t)

                def stream_scores(b, p, i):
                    pe.wait_ge(cache_in[p], 96 * i + 96)
                    pe.wait_ge(qx_ready, 4 * b + 4)
                    new = bass.ds(A_KEYS - P + b * FR, FR)
                    for keys, rhs in ((slice(0, CA), lambda j: ckT_sb[p][:, j, :]),
                                      (slice(CA, CA + FR), lambda j: k_win[:, j, new])):
                        for j in range(4):
                            mm = pe.matmul(PS[:, p, keys], qx_sb[p][:, j * P:(j + 1) * P], rhs(j),
                                           start=(j == 0), stop=(j == 3))
                    mm.then_inc(ds_psum, 1)
                    pe.matmul(PS[:, 2 + p, 0:CB], qxb_sb[p], ckbT_sb[p], start=True, stop=True)
                    pe.matmul(PS[:, 2 + p, CB:CB + FR], qxb_sb[p], kb_win[:, bass.ds(P + b * FR, FR)],
                              start=True, stop=True).then_inc(ds_psum, 1)

                def stream_values(b, p):
                    pe.wait_ge(dp_ready, 2 * b + 2)
                    pe.wait_ge(dpT_ready, 4 * b + CREDIT)
                    tr(4, 0, sc[p][:, 0:P])
                    tr(4, 1, sc[p][:, P:CA])
                    pe.transpose(PS[0:FR, 4, 2 * P:3 * P], sc[p][:, CA:CA + FR], ident)
                    tr(5, 0, sc[p][:, CA + FR:CA + FR + CB])
                    pe.transpose(PS[0:FR, 5, P:2 * P], sc[p][:, CA + FR + CB:CA + CB + 2 * FR], ident)\
                      .then_inc(dpT_psum, 1)
                    pe.wait_ge(dpT_ready, 4 * b + 4 + CREDIT)
                    pe.wait_ge(doT_ready, 4 * b + CREDIT)
                    for j in range(4):
                        out = PS[:, 6, 32 * j:32 * j + 32]
                        c = slice(32 * j, 32 * j + 32)
                        w = slice(j * P, (j + 1) * P)
                        for k in range(2):
                            pe.matmul(out, cv_sb[p][:, k, w], pT[p][:, k, c], start=(k == 0), stop=False)
                        pe.matmul(out, vnew_sb[p][0:FR, w], pT[p][0:FR, 2, c], start=False, stop=True)
                    pe.matmul(PS[:, 6, P:2 * P], cvb_sb[p], pT[p][:, 3, :], start=True, stop=False)
                    pe.matmul(PS[:, 6, P:2 * P], vnew_sb[p][0:FR, AW:AW + P], pT[p][0:FR, 4, :],
                              start=False, stop=True).then_inc(doT_psum, 1)

                pe.wait_ge(qkT_ready, 4 * NT_PROMPT + 4)
                pe.wait_ge(h_ready, 2 * NT_PROMPT + CREDIT)
                stream_scores(0, 0, 0)
                with pe.Fori(0, STREAMS // 2 - 1) as i:
                    stream_scores(2 * i + 1, 1, i)
                    stream_values(2 * i, 0)
                    stream_scores(2 * i + 2, 0, i + 1)
                    stream_values(2 * i + 1, 1)
                stream_scores(7, 1, 3)
                stream_values(6, 0)
                stream_values(7, 1)
                pe.wait_ge(doT_ready, 4 * STREAMS + CREDIT)
                for k in range(KD):
                    mm = tr(k // 4, k % 4, xT[:, k, :])
                mm.then_inc(do_psum, 1)
                out_project(NT_PROMPT)

        top[0] = shared_top
        uv = [carve(2 * D) for _ in range(RING)]
        x2 = [carve(D) for _ in range(2)]
        hb = [carve(D) for _ in range(2)]
        x2T = carve(KD, P)
        qT2 = carve(2 * QSP, P)
        s_sb = carve(16, P)
        s_left = carve(P)
        g2_bc = carve(D)
        gf_bc = carve(D)
        y_sb = carve(D)
        diag = carve(RING, P)
        rank = carve(CAND)
        onehot = carve(QSP * TOPK, CAND)
        sv = carve(16, TOPK)
        si_u = carve(16, TOPK).bitcast(U32)
        si = carve(16, TOPK)
        cand = carve(H, CAND)
        expert_of = carve(H, CAND)
        c_left = carve(CAND)
        fv = carve(H, TOPK)
        fi_u = carve(H, TOPK).bitcast(U32)
        fi = carve(H, TOPK)
        eidx = carve(SLOTS)
        expert_idx = [carve(SLOTS).bitcast(U32) for _ in range(2)]
        gate = [carve(SLOTS) for _ in range(2)]
        gden = carve(H)
        a_dot = [carve(GROUP) for _ in range(2)]
        a_gelu = [carve(GROUP) for _ in range(2)]
        wgt = [carve(GROUP) for _ in range(2)]
        ss2 = carve(2)
        rstd2 = carve(2)
        newton2 = carve(2, 1)

        bc_in = sem("bc_in")
        h_in = [sem(f"h_in{p}") for p in range(2)]
        rank_ready = sem("rank_ready")
        chain_b = sem("chain_b")
        gather_chain = sem("gather_chain")
        ss2_ready = sem("ss2_ready")
        rms2_ready = sem("rms2_ready")
        x2_ready = sem("x2_ready")
        x2T_psum = sem("x2T_psum")
        x2T_ready = sem("x2T_ready")
        q_psum = sem("q_psum")
        q_ready = sem("q_ready")
        key_psum = sem("key_psum")
        key_ready = sem("key_ready")
        g_shift = sem("g_shift")
        g_exp = sem("g_exp")
        routed = sem("routed")
        uv_in = [sem(f"uv_in{s}") for s in range(RING)]
        dots_ready = sem("dots_ready")
        gelu_ready = sem("gelu_ready")
        wgt_ready = sem("wgt_ready")
        diag_ready = sem("diag_ready")
        slot_used = sem("slot_used")
        ssf_ready = sem("ssf_ready")
        rmsf_ready = sem("rmsf_ready")
        opened = sem("opened")
        y_ready = sem("y_ready")
        y_stored = sem("y_stored")

        def pieces(run, route_part, finish):
            def tiles(t, u, p, more):
                for part in range(1, PARTS):
                    if more and part in ROUTE_AT:
                        route_part(t + 1, u + p, 1 - p, ROUTE_AT[part])
                    run(t, p, part)
                if more:
                    run(t + 1, 1 - p, 0)
                finish(t, p)

            def first():
                for piece in ROUTE_PIECES:
                    route_part(0, 0, 0, piece)
                run(0, 0, 0)
            return first, tiles

        with nc.Block() as block:

            @block.sync
            def _(sp):
                sp.dma_start(hb[0], h_dram[0:P, :]).then_inc(h_in[0], 16)
                sp.dma_start(g2_bc, g2[0:1, :].broadcast_to([P, D])).then_inc(bc_in, 16)
                sp.dma_start(gf_bc, gf[0:1, :].broadcast_to([P, D])).then_inc(bc_in, 16)
                sp.dma_start(hb[1], h_dram[P:2 * P, :]).then_inc(h_in[1], 16)

                def load_h(t, p):
                    sp.wait_ge(opened, t - 1)
                    sp.dma_start(hb[p], h_dram[bass.ds(t * P, P), :]).then_inc(h_in[p], 16)

                def store(t, dst):
                    sp.wait_ge(y_ready, t + 1 + Y_CREDIT)
                    sp.dma_start(dst, y_sb).then_inc(y_stored, 16)

                with sp.Fori(0, 3) as i:
                    for p in range(2):
                        t = 2 * i + p
                        load_h(t + 2, p)
                        store(t, y_p[bass.ds(t * P, P), :])
                load_h(NT_PROMPT, 0)
                store(6, y_p[6 * P:7 * P, :])
                store(7, y_p[7 * P:8 * P, :])
                store(NT_PROMPT, y_s)
                sp.wait_ge(y_stored, 16 * NT + 16 * CREDIT)

            @block.gpsimd
            def _(pool):
                pool.sem_inc(y_stored, 16 * CREDIT)
                pool.sem_inc(y_ready, Y_CREDIT)
                pool.iota(rank, pattern=[[1, CAND]], base=0, channel_multiplier=0,
                          allow_small_or_imprecise_dtypes=True).then_inc(rank_ready, 1)

                ch = Chain(pool, gather_chain)

                def gathers(t, p):
                    pool.wait_ge(routed, t + 1)
                    ch.pass_on()
                    for s in range(SLOTS):
                        r = s % RING
                        if s >= RING or not isinstance(t, int) or t > 0:
                            pool.wait_ge(slot_used, t * SLOTS + s - RING + 1)
                            ch.pass_on()
                        pool.indirect_dma_start(
                            out=uv[r], out_offset=None, in_=experts,
                            in_offset=bass.IndirectOffsetOnAxis(ap=expert_idx[p][:, s:s + 1], axis=0))\
                            .then_inc(uv_in[r], 16)
                    ch.restart()

                gathers(0, 0)
                gathers(1, 1)
                with pool.Fori(1, 4) as i:
                    for p in range(2):
                        gathers(2 * i + p, p)
                gathers(NT_PROMPT, 0)

            @block.scalar
            def _(act):
                def run(t, p, part):
                    for g in range(PER_PART // GROUP):
                        n = part * (PER_PART // GROUP) + g
                        q = n % 2
                        grp = t * (SLOTS // GROUP) + n
                        act.wait_ge(dots_ready, grp * GROUP + GROUP)
                        act.activation(a_gelu[q], a_dot[q], ACT.Gelu).then_inc(gelu_ready, 1)
                        act.wait_ge(wgt_ready, grp + 1)
                        for k in range(GROUP):
                            s = n * GROUP + k
                            if s >= RING or not isinstance(t, int) or t > 0:
                                act.wait_ge(slot_used, t * SLOTS + s - RING + 1)
                            act.activation(diag[:, s % RING, :], ident, ACT.Copy,
                                           scale=wgt[q][:, k:k + 1]).then_inc(diag_ready, 1)

                def route_part(t, u, p, part):
                    if part == 0:
                        act.wait_ge(h_in[p], 16 * u + 16)
                        act.activation(x2[p], hb[p], ACT.Square, accum_out=ss2[:, 0:1]).then_inc(ss2_ready, 1)
                        act.wait_ge(ss2_ready, t + 1)
                        act.activation(rstd2[:, 0:1], ss2[:, 0:1], ACT.Sqrt, bias=eps, scale=1.0 / D)\
                           .then_inc(rms2_ready, 1)
                    if part < H // QSP:
                        k = part
                        act.wait_ge(q_psum, 4 * t + k + 1)
                        act.copy(qT2.rearrange("p a b -> p (a b)"), PS[:, 6, :]).then_inc(q_ready, 1)
                        act.wait_ge(key_psum, 4 * t + k + 1)
                        act.copy(s_sb[:, 4 * k:4 * k + 4, :].rearrange("p a b -> p (a b)"), PS[:, 7, :])\
                           .then_inc(key_ready, 1)
                    if part == ROUTE_PIECES[-1]:
                        act.wait_ge(g_shift, t + 1)
                        act.activation(gate[p], gate[p], ACT.Exp).then_inc(g_exp, 1)

                def finish(t, p):
                    act.wait_ge(slot_used, (t + 1) * SLOTS)
                    act.wait_ge(y_stored, 16 * t + 16 * CREDIT)
                    act.activation(y_sb, PS[:, 2 * p:2 * p + 2, :].rearrange("p a b -> p (a b)"), ACT.Square,
                                   accum_out=ss2[:, 1:2]).then_inc(ssf_ready, 1)
                    act.wait_ge(ssf_ready, t + 1)
                    act.activation(rstd2[:, 1:2], ss2[:, 1:2], ACT.Sqrt, bias=eps, scale=1.0 / D)\
                       .then_inc(rmsf_ready, 1)

                first, tiles = pieces(run, route_part, finish)
                first()
                with act.Fori(0, 4) as i:
                    for p in range(2):
                        tiles(2 * i + p, i, p, True)
                tiles(NT_PROMPT, NT_PROMPT // 2, 0, False)

            @block.vector
            def _(dve):
                ch = Chain(dve, chain_b)

                def run(t, p, part):
                    for g in range(PER_PART // GROUP):
                        n = part * (PER_PART // GROUP) + g
                        q = n % 2
                        for k in range(GROUP):
                            s = n * GROUP + k
                            r = s % RING
                            dve.wait_ge(uv_in[r], 16 * (t * (SLOTS // RING) + s // RING + 1))
                            dve.tensor_tensor_reduce(uv[r][:, 0:D], uv[r][:, 0:D], x2[p], 1.0, 0.0, ALU.mult,
                                                     ALU.add, a_dot[q][:, k:k + 1])\
                               .then_inc(dots_ready, 1)
                        grp = t * (SLOTS // GROUP) + n
                        dve.wait_ge(gelu_ready, grp + 1)
                        dve.tensor_tensor(wgt[q], a_gelu[q], gate[p][:, n * GROUP:(n + 1) * GROUP], ALU.mult)\
                           .then_inc(wgt_ready, 1)

                def top16(values, left, src, idx):
                    ch.mark(dve.max(values[:, 0:8], src))
                    ch.settle()
                    ch.mark(dve.match_replace(left, values[:, 0:8], src, LOWEST))
                    ch.mark(dve.max_index(idx[:, 0:8], values[:, 0:8], src))
                    ch.settle()
                    ch.mark(dve.max(values[:, 8:16], left))
                    ch.settle()
                    ch.mark(dve.max_index(idx[:, 8:16], values[:, 8:16], left))

                def route_part(t, u, p, part):
                    if part == 0:
                        dve.wait_ge(rms2_ready, t + 1)
                        invert_rms(dve, ch, rstd2[:, 0:1], ss2[:, 0:1], newton2, D)
                        dve.scalar_tensor_tensor(out=x2[p], in0=hb[p], scalar=rstd2[:, 0:1], in1=g2_bc,
                                                 op0=ALU.mult, op1=ALU.mult).then_inc(x2_ready, 1)
                        dve.wait_ge(x2T_psum, t + 1)
                        dve.tensor_copy(x2T.rearrange("p a b -> p (a b)"),
                                        PS[:, 4:6, :].rearrange("p a b -> p (a b)")).then_inc(x2T_ready, 1)
                    if 1 <= part <= H // QSP:
                        k = part - 1
                        dve.wait_ge(key_ready, 4 * t + k + 1)
                        ch.pass_on()
                        for l in range(4 * k, 4 * k + 4):
                            top16(sv[:, l, :], s_left, s_sb[:, l, :], si_u[:, l, :])
                    if part == 5:
                        ch.settle()
                        ch.mark(dve.tensor_copy(si, si_u))
                        ch.settle()
                        si4 = si.rearrange("p (h two) k -> p h two k", two=2)
                        sv4 = sv.rearrange("p (h two) k -> p h two k", two=2)
                        ch.mark(dve.tensor_scalar(si4[:, :, 0, :], si4[:, :, 0, :], float(NKEYS), None, ALU.mult))
                        ch.settle()
                        at = 0
                        for i, w in enumerate(ROWS):
                            if w == 1 and i and ROWS[i - 1] == 1:
                                continue
                            n = ROWS.count(1) if w == 1 else 1
                            for dst, v4 in ((cand, sv4), (expert_of, si4)):
                                if w == 1:
                                    a = v4[:, :, 0, i:i + n]
                                    b = v4[:, :, 1, 0:1].broadcast_to([P, H, n])
                                else:
                                    a = v4[:, :, 0, i:i + 1].broadcast_to([P, H, w])
                                    b = v4[:, :, 1, 0:w]
                                ch.mark(dve.tensor_tensor(dst[:, :, at:at + w * n], a, b, ALU.add))
                            at += w * n
                        assert at == CAND
                        ch.settle()
                    if part in BEST_OF_SUMS:
                        for h in BEST_OF_SUMS[part]:
                            top16(fv[:, h, :], c_left, cand[:, h, :], fi_u[:, h, :])
                        ch.settle()
                    if 8 <= part < 12:
                        k = part - 8
                        if k == 0:
                            ch.mark(dve.tensor_copy(fi, fi_u))
                            ch.settle()
                        oh = onehot.rearrange("p (h k) c -> p h k c", h=QSP)
                        for h in range(QSP):
                            ch.mark(dve.tensor_tensor(
                                oh[:, h], rank.unsqueeze(1).broadcast_to([P, TOPK, CAND]),
                                fi[:, QSP * k + h, :].unsqueeze(2).broadcast_to([P, TOPK, CAND]), ALU.is_equal))
                        ch.settle()
                        for h in range(QSP):
                            ch.mark(dve.tensor_tensor(
                                oh[:, h], oh[:, h],
                                expert_of[:, QSP * k + h, :].unsqueeze(1).broadcast_to([P, TOPK, CAND]), ALU.mult))
                        ch.settle()
                        ch.mark(dve.tensor_reduce(eidx[:, QSP * TOPK * k:QSP * TOPK * (k + 1)], onehot, AX_X,
                                                  ALU.add))
                        ch.settle()
                    if part == 11:
                        dve.tensor_copy(expert_idx[p], eidx).then_inc(routed, 1)
                        g3 = gate[p].rearrange("p (h k) -> p h k", h=H)
                        dve.tensor_tensor(g3, fv, fv[:, :, 0:1].broadcast_to([P, H, TOPK]), ALU.subtract)\
                           .then_inc(g_shift, 1)
                    if part == 12:
                        g3 = gate[p].rearrange("p (h k) -> p h k", h=H)
                        dve.wait_ge(g_exp, t + 1)
                        ch.mark(dve.tensor_reduce(gden, g3, AX_X, ALU.add))
                        ch.settle()
                        ch.mark(dve.reciprocal(gden, gden))
                        ch.settle()
                        ch.mark(dve.tensor_tensor(g3, g3, gden.unsqueeze(2).broadcast_to([P, H, TOPK]), ALU.mult))
                        ch.restart()

                def finish(t, p):
                    dve.wait_ge(rmsf_ready, t + 1)
                    invert_rms(dve, ch, rstd2[:, 1:2], ss2[:, 1:2], newton2, D)
                    ch.restart()
                    dve.scalar_tensor_tensor(out=y_sb, in0=PS[:, 2 * p:2 * p + 2, :].rearrange("p a b -> p (a b)"),
                                             scalar=rstd2[:, 1:2], in1=gf_bc, op0=ALU.mult, op1=ALU.mult)\
                       .then_inc(y_ready, 1)

                dve.wait_ge(bc_in, 32)
                dve.wait_ge(rank_ready, 1)
                first, tiles = pieces(run, route_part, finish)
                first()
                with dve.Fori(0, 4) as i:
                    for p in range(2):
                        tiles(2 * i + p, i, p, True)
                tiles(NT_PROMPT, NT_PROMPT // 2, 0, False)

            @block.tensor
            def _(pe):
                def run(t, p, part):
                    if part == 0:
                        pe.wait_ge(y_ready, t - 1 + Y_CREDIT)
                        for c in range(2):
                            mm = pe.matmul(PS[:, 2 * p + c, :], ident, hb[p][:, 512 * c:512 * c + 512],
                                           start=True, stop=False)
                        mm.then_inc(opened, 1)
                    for s in range(part * PER_PART, (part + 1) * PER_PART):
                        r = s % RING
                        pe.wait_ge(diag_ready, t * SLOTS + s + 1)
                        for c in range(2):
                            mm = pe.matmul(PS[:, 2 * p + c, :], diag[:, r, :],
                                           uv[r][:, D + 512 * c:D + 512 * c + 512], start=False,
                                           stop=(s == SLOTS - 1))
                        mm.then_inc(slot_used, 1)

                def route_part(t, u, p, part):
                    if part == 0:
                        pe.wait_ge(x2_ready, t + 1)
                        for k in range(KD):
                            mm = pe.transpose(PS[:, 4 + k // 4, (k % 4) * P:(k % 4 + 1) * P],
                                              x2[p][:, k * P:(k + 1) * P], ident)
                        mm.then_inc(x2T_psum, 1)
                        pe.wait_ge(x2T_ready, t + 1)
                    if part < H // QSP:
                        for l in range(4):
                            c = (4 * part + l) * P
                            for k in range(KD):
                                mm = pe.matmul(PS[:, 6, l * P:(l + 1) * P], w_query_sb[:, k, c:c + P], x2T[:, k, :],
                                               start=(k == 0), stop=(k == KD - 1))
                        mm.then_inc(q_psum, 1)
                        pe.wait_ge(q_ready, 4 * t + part + 1)
                        for l in range(4):
                            mm = pe.matmul(PS[:, 7, l * P:(l + 1) * P], qT2[:, l, :], subk_sb[:, 4 * part + l, :],
                                           start=True, stop=True)
                        mm.then_inc(key_psum, 1)

                def finish(t, p):
                    pass

                pe.wait_ge(w_query_ready, 32)
                first, tiles = pieces(run, route_part, finish)
                first()
                with pe.Fori(0, 4) as i:
                    for p in range(2):
                        tiles(2 * i + p, i, p, True)
                tiles(NT_PROMPT, NT_PROMPT // 2, 0, False)


def kernel(x_prompt, x_sample, cache_a_k, cache_a_v, cache_b_k, cache_b_v, norm1_g, w_in, rel_bias, sinks,
           out_norm_a_g, out_norm_b_g, w_out, norm2_g, w_query, sub_keys, expert_u, expert_v, norm_f_g):
    import numpy as np
    import concourse.bacc as bacc
    from concourse import mybir as mb
    from concourse.bass_utils import run_bass_kernel_spmd as run

    rel = np.asarray(rel_bias)[0]
    dist = 512 + np.arange(128)[:, None] - np.arange(640)[None, :]
    bias_a = rel[:, np.clip(dist, -63, 256) + 63].transpose(1, 0, 2)
    dist_s = 256 + np.arange(16)[:, None] - np.arange(272)[None, :]
    bias_sa = rel[:, np.clip(dist_s, -63, 256) + 63].reshape(128, 272)
    slope = 2.0 ** -np.arange(1, 9, dtype=np.float32)
    q, c = np.arange(128)[:, None], np.arange(256)[None, :]
    outside = (c // 64 < q // 64) | (c // 64 > q // 64 + 2)
    bias_b = np.where(outside[:, None, :], np.float32(-1e30),
                      -slope[None, :, None] * np.abs(128 + q - c).astype(np.float32)[:, None, :]).astype(np.float32)
    kpos = np.abs(128 + np.arange(16)[:, None] - np.arange(144)[None, :]).astype(np.float32)
    bias_sb = (-slope[:, None, None] * kpos[None]).reshape(128, 144).astype(np.float32)
    w = np.asarray(w_in)[0]
    qb = w[:, 1536:2048].reshape(1024, 2, 4, 64).transpose(0, 2, 1, 3).reshape(1024, 512)
    w = np.concatenate([w[:, :1536], qb, w[:, 2048:]], axis=1)
    ck = np.asarray(cache_a_k)[0].transpose(0, 2, 3, 1).reshape(8, 4, 128, 256).transpose(0, 2, 1, 3)
    arrays = {
        "x_prompt": np.asarray(x_prompt).reshape(1024, 1024),
        "x_sample": np.asarray(x_sample).reshape(128, 1024),
        "ckT": ck.reshape(1024, 1024),
        "cv": np.asarray(cache_a_v)[0].reshape(8 * 256, 512),
        "ckbT": np.asarray(cache_b_k)[0].transpose(0, 2, 3, 1).reshape(8 * 128, 128),
        "cvb": np.asarray(cache_b_v)[0].reshape(8 * 128, 128),
        "g1": np.asarray(norm1_g)[0].reshape(8, 128).T,
        "w_in": w,
        "bias_a": bias_a, "bias_b": bias_b, "bias_sa": bias_sa, "bias_sb": bias_sb,
        "sinks": np.asarray(sinks),
        "sink_rows": np.repeat(np.asarray(sinks)[0], 16).reshape(128, 1),
        "g_ab": np.concatenate([np.asarray(out_norm_a_g)[0], np.asarray(out_norm_b_g)[0]]).reshape(8, 128).T,
        "w_out": np.asarray(w_out)[0],
        "g2": np.asarray(norm2_g),
        "w_query": np.asarray(w_query)[0],
        "subk": np.asarray(sub_keys)[0].transpose(3, 0, 1, 2).reshape(128, 2048),
        "experts": np.concatenate([np.asarray(expert_u)[0], np.asarray(expert_v)[0]], axis=1),
        "gf": np.asarray(norm_f_g).reshape(1, 1024),
    }
    nc = bacc.Bacc("TRN2", target_bir_lowering=False, num_devices=1)
    ins, sent = [], {}
    for name, a in arrays.items():
        a = np.ascontiguousarray(a)
        sent[f"in_{name}"] = a
        ins.append(nc.dram_tensor(f"in_{name}", a.shape, mb.dt.from_np(a.dtype), kind="ExternalInput").ap())
    shapes = [(1024, 1024), (128, 1024), (512, 512), (512, 512), (128, 128), (128, 128),
              (128, 512), (128, 512), (128, 128), (128, 128)]
    outs = [nc.dram_tensor(f"out_{i}", s, mb.dt.float32, kind="ExternalOutput").ap() for i, s in enumerate(shapes)]
    build(nc, ins, outs)
    r = run(nc, [sent], core_ids=[0]).results[0]
    final = [(1, 1024, 1024), (8, 16, 1024), (1, 1, 512, 8, 64), (1, 1, 512, 8, 64), (1, 1, 128, 2, 64),
             (1, 1, 128, 2, 64), (1, 8, 16, 8, 64), (1, 8, 16, 8, 64), (1, 8, 16, 2, 64), (1, 8, 16, 2, 64)]
    return tuple(np.asarray(r[f"out_{i}"]).reshape(s) for i, s in enumerate(final))
```

```python
import concourse.bass as bass
from concourse import mybir
from concourse.alu_op_type import AluOpType as ALU
from contextlib import ExitStack

F32 = mybir.dt.float32
U32 = mybir.dt.uint32
ACT = mybir.ActivationFunctionType
AX_X = mybir.AxisListType.X

P = 128
D = 1024
KD = D // P
HD = 64
H = 8
AW = H * HD
NT_PROMPT = 8
NT = 9
W_IN = 3 * AW + AW + 4 * HD
A_BLK = 5
A_KEYS = A_BLK * P
B_KEYS = 2 * P
STREAMS = 8
FR = 16
CA = 256
CB = 128
EPS = 1e-6
SCALE = HD ** -0.5
NEG = -1e30
LOWEST = -3.0e38
NKEYS = 128
TOPK = 16
ROWS = [TOPK // (i + 1) for i in range(TOPK)]
CAND = sum(ROWS)
SLOTS = H * TOPK
RING = 8
GROUP = 2
QSP = 2
PARTS = 16
PER_PART = SLOTS // PARTS
PAIRS = H // QSP
AHEAD = 4
ROUTE_AT = {4: [("keys", 0)], 5: [("halves", 0)], 6: [("keys", 1), ("sums", 0)], 7: [("halves", 1)],
            8: [("keys", 2), ("experts", 0)], 9: [("halves", 2)], 10: [("keys", 3), ("sums", 1)],
            11: [("halves", 3)], 12: [("experts", 1), ("sums", 2)], 13: [("experts", 2)],
            14: [("sums", 3)], 15: [("experts", 3), ("gates", 0, PAIRS)]}
FIRST = [("keys", 0), ("halves", 0), ("keys", 1), ("sums", 0), ("experts", 0), ("gates", 0, 1), ("keys", 2),
         ("halves", 1), ("sums", 1), ("keys", 3), ("experts", 1), ("gates", 1, 1), 0, ("halves", 2),
         ("sums", 2), ("experts", 2), ("gates", 2, 1), 1, ("halves", 3), ("sums", 3), ("experts", 3),
         ("gates", 3, 1), 2, 3]
ARENA = 53000
Y_CREDIT = 2
CREDIT = 1


def item_parts(n):
    return 2 * (n + 1) if n < H else 2 * H + n - H + 1


TILE_PARTS = item_parts(15)


class Chain:

    def __init__(self, eng, sem):
        self.eng, self.sem, self.n = eng, sem, 0

    def restart(self):
        self.settle()
        self.eng.sem_clear(self.sem)
        self.n = 0

    def mark(self, ins):
        ins.then_inc(self.sem, 1)
        self.n += 1

    def pass_on(self):
        self.eng.sem_inc(self.sem, 1)
        self.n += 1
        self.settle()

    def settle(self):
        self.eng.wait_ge(self.sem, self.n)




def invert_rms(dve, ch, r, squares, tmp, width):
    v, q = tmp[:, 0, :], tmp[:, 1, :]
    ch.mark(dve.tensor_scalar(v, squares, 1.0 / width, EPS, ALU.mult, ALU.add))
    ch.mark(dve.reciprocal(r, r))
    ch.settle()
    ch.mark(dve.tensor_tensor(q, r, r, ALU.mult))
    ch.settle()
    ch.mark(dve.tensor_tensor(q, q, v, ALU.mult))
    ch.settle()
    ch.mark(dve.tensor_scalar(q, q, -0.5, 1.5, ALU.mult, ALU.add))
    ch.settle()
    ch.mark(dve.tensor_tensor(r, r, q, ALU.mult))
    ch.settle()


def build(nc, ins, outs):
    (x_prompt, x_sample, ckT, cv, ckbT, cvb, g1, w_in, bias_a, bias_b, bias_sa, bias_sb, sinks, sink_rows,
     g_ab, w_out, g2, w_query, subk, experts, gf) = ins
    (y_p, y_s, ak_p, av_p, bk_p, bv_p, ak_s, av_s, bk_s, bv_s) = outs
    h_dram = nc.dram_tensor("h_scratch", (NT * P, D), F32, kind="Internal").ap()

    ctx = ExitStack()
    with ctx:
        def sem(name):
            return ctx.enter_context(nc.semaphore(name))

        PS = ctx.enter_context(nc.psum_tensor("PS", [P, 8, 512], F32))
        ident_t = ctx.enter_context(nc.sbuf_tensor("ident", [P, P], F32))
        ident = ident_t[:, :]
        eps = ctx.enter_context(nc.sbuf_tensor("eps", [P, 1], F32))[:, :]
        arena_t = ctx.enter_context(nc.sbuf_tensor("arena", [P, ARENA], F32))
        w_query_ready = sem("w_query_ready")
        ident_ready = sem("ident_ready")

        top = [0]

        def carve(*shape):
            n = 1
            for s in shape:
                n *= s
            v = arena_t[:, top[0]:top[0] + n]
            top[0] += n
            assert top[0] <= ARENA, top[0]
            if len(shape) == 2:
                v = v.rearrange("p (a b) -> p a b", a=shape[0])
            return v

        w_in_sb = carve(KD, W_IN)
        w_query_sb = arena_t[:, 0:KD * 2048].rearrange("p (a b) -> p a b", a=KD)
        subk_sb = arena_t[:, KD * 2048:KD * 2048 + 16 * P].rearrange("p (a b) -> p a b", a=16)
        shared_top = top[0]

        w_out_sb = carve(KD, D)
        overlay = top[0]
        bias_a_sb = carve(H, A_KEYS)
        bias_b_sb = carve(H, B_KEYS)
        end_overlay = top[0]
        top[0] = overlay
        ckT_sb = [carve(4, CA) for _ in range(2)]
        cv_sb = [carve(2, AW) for _ in range(2)]
        ckbT_sb = [carve(CB) for _ in range(2)]
        cvb_sb = [carve(P) for _ in range(2)]
        vnew_sb = [carve(AW + P) for _ in range(2)]
        qx_sb = [carve(640) for _ in range(2)]
        assert top[0] <= end_overlay, (top[0], end_overlay)
        top[0] = end_overlay
        qxb_sb = [carve(P) for _ in range(2)]
        bias_sa_sb = carve(CA + FR)
        bias_sb_sb = carve(CB + FR)
        k_win = carve(4, A_KEYS)
        v_win = carve(A_BLK, AW)
        kb_win = carve(B_KEYS)
        vb_win = carve(2, P)
        valid = carve(A_KEYS)
        x_sb = [carve(D) for _ in range(2)]
        xn = carve(D)
        xT = carve(KD, P)
        o_sb = carve(D)
        oT = carve(KD, P)
        z = carve(W_IN)
        qT = carve(8, P)
        sc = [carve(A_KEYS) for _ in range(2)]
        pT = [carve(A_BLK, P) for _ in range(2)]
        g1_sb = carve(KD)
        g_ab_sb = carve(KD)
        sink_sb = carve(H + 1)
        ss = carve(4)
        rstd = carve(4)
        newton = carve(2, 2)
        m_sb = carve(16)
        nm = carve(16)
        den = carve(16)
        rcp = carve(16)
        sd = carve(H)
        es = carve(H)
        m_s = [carve(2) for _ in range(2)]
        nm_s = [carve(2) for _ in range(2)]
        sd_s = [carve(1) for _ in range(2)]
        den_s = [carve(2) for _ in range(2)]
        es_s = [carve(1) for _ in range(2)]
        rcp_s = [carve(2) for _ in range(2)]
        VA, KB = slice(2 * AW, 3 * AW), slice(4 * AW, 4 * AW + P)
        VB = slice(4 * AW + P, W_IN)

        S_BANK = (0, 1)
        S_OWN = 2
        PT_BANK = (3, 4)
        PT_OWN = 5
        OA_BANK = 6
        OB_BANK = 5
        UNIT = 7

        const_in = sem("const_in")
        g1_in = sem("g1_in")
        w_in_in = [sem(f"w_in_in{c}") for c in range(5)]
        w_out_in = sem("w_out_in")
        x_in = [sem(f"x_in{p}") for p in range(2)]
        windows_clear = sem("windows_clear")
        pool_chain = sem("pool_chain")
        dve_chain = sem("dve_chain")
        ss_ready = sem("ss_ready")
        rms_ready = sem("rms_ready")
        xn_ready = sem("xn_ready")
        xT_psum = sem("xT_psum")
        xT_ready = sem("xT_ready")
        proj_psum = sem("proj_psum")
        z_ready = sem("z_ready")
        z_free = sem("z_free")
        kv_stored = sem("kv_stored")
        shifted = sem("shifted")
        qkT_psum = sem("qkT_psum")
        qkT_ready = sem("qkT_ready")
        s_psum = sem("s_psum")
        s_read = sem("s_read")
        nm_ready = sem("nm_ready")
        e_ready = sem("e_ready")
        pT_psum = sem("pT_psum")
        pT_ready = sem("pT_ready")
        o_psum = sem("o_psum")
        sd_ready = sem("sd_ready")
        es_ready = sem("es_ready")
        o_ready = sem("o_ready")
        sso_ready = sem("sso_ready")
        rmso_ready = sem("rmso_ready")
        on_ready = sem("on_ready")
        oT_psum = sem("oT_psum")
        oT_ready = sem("oT_ready")
        wo_psum = sem("wo_psum")
        h_ready = sem("h_ready")
        h_stored = sem("h_stored")
        new_kv_stored = sem("new_kv_stored")
        cache_k_in = [sem(f"cache_k_in{p}") for p in range(2)]
        cache_v_in = [sem(f"cache_v_in{p}") for p in range(2)]
        qx_clear = sem("qx_clear")
        qx_ready = sem("qx_ready")
        ds_psum = sem("ds_psum")
        dnm_ready = sem("dnm_ready")
        de_ready = sem("de_ready")
        dp_ready = sem("dp_ready")
        dpT_psum = sem("dpT_psum")
        dpT_ready = sem("dpT_ready")
        doT_psum = sem("doT_psum")
        doT_ready = sem("doT_ready")
        do_psum = sem("do_psum")

        NORM_AT = 1
        PIECE_AT = {2: 0, 3: 1, 5: 2, 7: 3, 10: 4, 13: 5}
        LAST_PIECE = 6
        PIECES = range(LAST_PIECE + 1)
        BLOCKS = (0, 1, 3, 4, 2)

        def gcol(g, n):
            return g.unsqueeze(2).broadcast_to([P, n, P])

        with nc.Block() as block:

            @block.sync
            def _(sp):
                sp.dma_start(x_sb[0], x_prompt[0:P, :]).then_inc(x_in[0], 16)
                w_v = w_in.rearrange("(k p) n -> p k n", p=P)
                sp.dma_start(g1_sb, g1).then_inc(g1_in, 16)
                for c in BLOCKS:
                    cols = slice(512 * c, min(512 * c + 512, W_IN))
                    sp.dma_start(w_in_sb[:, :, cols], w_v[:, :, cols]).then_inc(w_in_in[c], 16)
                sp.dma_start(x_sb[1], x_prompt[P:2 * P, :]).then_inc(x_in[1], 16)
                sp.dma_start(g_ab_sb, g_ab).then_inc(const_in, 16)
                sp.dma_start(sink_sb[:, 0:H], sinks[0:1, :].broadcast_to([P, H])).then_inc(const_in, 16)
                sp.dma_start(sink_sb[:, H:H + 1], sink_rows).then_inc(const_in, 16)
                sp.dma_start(bias_a_sb, bias_a).then_inc(const_in, 16)
                sp.dma_start(bias_b_sb, bias_b).then_inc(const_in, 16)
                sp.dma_start(bias_sa_sb, bias_sa).then_inc(const_in, 16)
                sp.dma_start(bias_sb_sb, bias_sb).then_inc(const_in, 16)
                sp.dma_start(w_out_sb, w_out.rearrange("(k p) n -> p k n", p=P)).then_inc(w_out_in, 16)

                def store_h(t, p):
                    sp.wait_ge(h_ready, 2 * t + 2 + CREDIT)
                    sp.dma_start(h_dram[bass.ds(t * P, P), :], x_sb[p]).then_inc(h_stored, 16)
                    sp.wait_ge(h_stored, 16 * t + 16)

                with sp.Fori(0, 2) as i:
                    for p in range(2):
                        sp.sem_inc(z_free, 1)
                        store_h(2 * i + p, p)
                        sp.dma_start(x_sb[p], x_prompt[bass.ds((2 * i + p + 2) * P, P), :])\
                          .then_inc(x_in[p], 16)
                for t in range(4, NT_PROMPT):
                    p = t % 2
                    rows = slice((t - 4) * P, (t - 3) * P)
                    sp.wait_ge(z_ready, 5 * t + 5)
                    sp.dma_start(ak_p[rows, :], z[:, AW:2 * AW]).then_inc(kv_stored, 16)
                    sp.dma_start(av_p[rows, :], z[:, VA]).then_inc(kv_stored, 16)
                    if t == NT_PROMPT - 1:
                        sp.dma_start(bk_p, z[:, KB]).then_inc(kv_stored, 16)
                        sp.dma_start(bv_p, z[:, VB]).then_inc(kv_stored, 16)
                    sp.wait_ge(kv_stored, 32 * (t - 3) + (32 if t == NT_PROMPT - 1 else 0))
                    sp.sem_inc(z_free, 1)
                    if t == NT_PROMPT - 1:
                        break
                    store_h(t, p)
                    if t + 2 < NT_PROMPT:
                        sp.dma_start(x_sb[p], x_prompt[(t + 2) * P:(t + 3) * P, :]).then_inc(x_in[p], 16)
                    elif t + 2 == NT_PROMPT:
                        sp.dma_start(x_sb[p], x_sample).then_inc(x_in[p], 16)

                t = NT_PROMPT
                sp.wait_ge(z_ready, 5 * t + 5)
                sp.dma_start(ak_s, z[:, AW:2 * AW]).then_inc(new_kv_stored, 16)
                sp.dma_start(av_s, z[:, VA]).then_inc(new_kv_stored, 16)
                sp.dma_start(bk_s, z[:, KB]).then_inc(new_kv_stored, 16)
                sp.dma_start(bv_s, z[:, VB]).then_inc(new_kv_stored, 16)
                def load_keys(b, p):
                    q = cache_k_in[p]
                    sp.dma_start(ckT_sb[p].rearrange("p a b -> p (a b)"),
                                 ckT[bass.ds(b * P, P), :]).then_inc(q, 16)
                    sp.dma_start(ckbT_sb[p], ckbT[bass.ds(b * P, P), :]).then_inc(q, 16)

                def load_values(b, p):
                    q = cache_v_in[p]
                    sp.dma_start(cv_sb[p], cv[bass.ds(b * CA, CA), :]
                                 .rearrange("(a p) c -> p a c", p=P)).then_inc(q, 16)
                    sp.dma_start(cvb_sb[p], cvb[bass.ds(b * P, P), :]).then_inc(q, 16)
                    sp.dma_start(vnew_sb[p][0:FR, 0:AW], av_s[bass.ds(b * FR, FR), :]).then_inc(q, 16)
                    sp.dma_start(vnew_sb[p][0:FR, AW:AW + P], bv_s[bass.ds(b * FR, FR), :]).then_inc(q, 16)

                sp.wait_ge(nm_ready, 16 * NT_PROMPT)
                load_keys(0, 0)
                load_keys(1, 1)
                sp.wait_ge(new_kv_stored, 64)
                load_values(0, 0)
                load_values(1, 1)

                def load_query_weights(k):
                    sp.dma_start(w_query_sb[:, k, :], w_query[k * P:(k + 1) * P, :]).then_inc(w_query_ready, 16)

                load_query_weights(0)
                load_query_weights(1)
                store_h(NT_PROMPT - 1, 1)
                for b in range(2, STREAMS):
                    sp.wait_ge(ds_psum, 2 * b - 2 + CREDIT)
                    load_keys(b, b % 2)
                    sp.wait_ge(doT_psum, b - 1)
                    load_values(b, b % 2)
                    load_query_weights(b)
                sp.dma_start(subk_sb.rearrange("p a b -> p (a b)"), subk).then_inc(w_query_ready, 16)
                store_h(t, 0)

            @block.gpsimd
            def _(pool):
                for ahead in (z_free, o_psum, h_ready, dpT_ready, doT_ready, ds_psum, sso_ready, shifted):
                    pool.sem_inc(ahead, CREDIT)
                ch = Chain(pool, pool_chain)
                ch.mark(pool.memset(ident, 0.0))
                ch.settle()
                pool.memset(eps, EPS).then_inc(ident_ready, 1)
                pool.affine_select(out=ident, in_=ident, compare_op=ALU.not_equal, fill=1.0, base=0,
                                   pattern=[[-1, P]], channel_multiplier=1).then_inc(ident_ready, 1)
                k2 = k_win.rearrange("p a b -> p (a b)")
                v2 = v_win.rearrange("p a b -> p (a b)")
                vb2 = vb_win.rearrange("p a b -> p (a b)")
                for w in (k2, v2, kb_win, vb2):
                    ch.mark(pool.memset(w, 0.0))
                ch.mark(pool.memset(valid, NEG))
                ch.settle()

                def shift(t):
                    pool.wait_ge(o_psum, 16 * t + CREDIT)
                    ch.pass_on()
                    for blk in range(A_BLK - 1):
                        a, b = blk * P, (blk + 1) * P
                        ch.mark(pool.tensor_copy(k_win[:, :, a:b], k_win[:, :, a + P:b + P]))
                        ch.mark(pool.tensor_copy(v_win[:, blk, :], v_win[:, blk + 1, :]))
                        ch.mark(pool.tensor_copy(valid[:, a:b], valid[:, a + P:b + P]))
                        if blk == 0:
                            ch.mark(pool.tensor_copy(kb_win[:, 0:P], kb_win[:, P:2 * P]))
                            ch.mark(pool.tensor_copy(vb_win[:, 0, :], vb_win[:, 1, :]))
                        ch.settle()
                    ch.mark(pool.memset(valid[:, A_KEYS - P:A_KEYS], 0.0))
                    pool.wait_ge(z_ready, 5 * t + 5)
                    ch.pass_on()
                    ch.mark(pool.tensor_copy(v_win[:, A_BLK - 1, :], z[:, VA]))
                    ch.settle()
                    pool.tensor_copy(vb_win[:, 1, :], z[:, VB]).then_inc(shifted, 1)
                    ch.restart()

                shift(0)
                pool.wait_ge(const_in, 16 * 7)
                ch.settle()
                pool.memset(bias_a_sb[0:64, :, A_KEYS - 64:A_KEYS], NEG).then_inc(windows_clear, 1)
                pool.wait_ge(windows_clear, 1)
                pool.memset(bias_a_sb[64:P, :, 0:64], NEG).then_inc(windows_clear, 1)
                pool.wait_ge(windows_clear, 2)
                with pool.Fori(1, NT) as t:
                    shift(t)
                pool.wait_ge(nm_ready, 16 * NT_PROMPT)
                for p in range(2):
                    pool.memset(qx_sb[p], 0.0).then_inc(qx_clear, 1)
                    pool.memset(qxb_sb[p], 0.0).then_inc(qx_clear, 1)

            @block.scalar
            def _(act):
                def norm(t, u, p):
                    act.wait_ge(x_in[p], 16 * u + 16)
                    act.activation(xn, x_sb[p], ACT.Square, accum_out=ss[:, 0:1]).then_inc(ss_ready, 1)
                    act.wait_ge(ss_ready, t + 1)
                    act.activation(rstd[:, 0:1], ss[:, 0:1], ACT.Sqrt, bias=eps, scale=1.0 / D)\
                       .then_inc(rms_ready, 1)

                def piece(t, k):
                    if k < 2:
                        return
                    c = BLOCKS[k - 2]
                    if k == 2:
                        act.wait_ge(z_free, t + CREDIT)
                        act.wait_ge(shifted, t + CREDIT)
                    act.wait_ge(proj_psum, 5 * t + k - 1)
                    w = min(512, W_IN - 512 * c)
                    act.copy(z[:, 512 * c:512 * c + w], PS[:, UNIT, 0:w]).then_inc(z_ready, 1)

                def queries_T(t):
                    for n, (bank, half) in enumerate(((0, 0), (2, 4))):
                        act.wait_ge(qkT_psum, 4 * t + n + 1)
                        act.mul(qT[:, half:half + 4, :].rearrange("p a b -> p (a b)"), PS[:, bank, :], SCALE)\
                           .then_inc(qkT_ready, 1)

                def keys_T(t):
                    act.wait_ge(qkT_psum, 4 * t + 3)
                    act.wait_ge(shifted, t + 1 + CREDIT)
                    act.copy(k_win[:, :, A_KEYS - P:A_KEYS],
                             PS[:, 1, :].rearrange("p (a b) -> p a b", a=4)).then_inc(qkT_ready, 1)
                    act.wait_ge(qkT_psum, 4 * t + 4)
                    act.copy(kb_win[:, P:2 * P], PS[:, 3, 0:P]).then_inc(qkT_ready, 1)

                def out_squares(t):
                    act.wait_ge(o_ready, 2 * t + 2)
                    act.activation(sc[0][:, 0:AW], o_sb[:, 0:AW], ACT.Square,
                                   accum_out=ss[:, 1:2]).then_inc(sso_ready, 1)
                    act.activation(sc[1][:, 0:AW], o_sb[:, AW:D], ACT.Square,
                                   accum_out=ss[:, 2:3]).then_inc(sso_ready, 1)
                    act.wait_ge(sso_ready, 2 * t + 2 + CREDIT)
                    act.activation(rstd[:, 1:3], ss[:, 1:3], ACT.Sqrt, bias=eps, scale=1.0 / AW)\
                       .then_inc(rmso_ready, 1)

                def evacuate_pT(t, n):
                    q = n % 2
                    act.wait_ge(pT_psum, 16 * t + n + 1)
                    if n >= 2:
                        act.wait_ge(o_psum, 16 * t + n - 1 + CREDIT)
                    w = 2
                    if n < H:
                        act.copy(pT[q][:, 4, :], PS[:, PT_OWN, 0:P]).then_inc(pT_ready, 1)
                        w = 4
                    act.copy(pT[q][:, 0:w, :].rearrange("p a b -> p (a b)"),
                             PS[:, PT_BANK[q], 0:w * P]).then_inc(pT_ready, 1)

                act.wait_ge(ident_ready, 2)
                norm(0, 0, 0)
                for k in PIECES:
                    piece(0, k)
                queries_T(0)
                keys_T(0)
                with act.Fori(0, NT_PROMPT // 2) as i:
                    for p in range(2):
                        t = 2 * i + p
                        for n in range(16):
                            w = A_KEYS if n < H else B_KEYS
                            act.wait_ge(nm_ready, 16 * t + n + 1)
                            act.activation(sc[n % 2][:, 0:w], sc[n % 2][:, 0:w], ACT.Exp, bias=nm[:, n:n + 1],
                                           accum_out=den[:, n:n + 1]).then_inc(e_ready, 1)
                            if n:
                                evacuate_pT(t, n - 1)
                            if n == NORM_AT:
                                norm(t + 1, i + p, 1 - p)
                            if n - 1 in PIECE_AT:
                                piece(t + 1, PIECE_AT[n - 1])
                        evacuate_pT(t, 15)
                        act.wait_ge(sd_ready, t + 1)
                        act.activation(es, sd, ACT.Exp).then_inc(es_ready, 1)
                        queries_T(t + 1)
                        out_squares(t)
                        piece(t + 1, LAST_PIECE)
                        keys_T(t + 1)

                def stream(b, p):
                    s = sc[p]
                    act.wait_ge(dnm_ready, 3 * b + 1)
                    act.activation(s[:, 0:CA + FR], s[:, 0:CA + FR], ACT.Exp, bias=nm_s[p][:, 0:1],
                                   accum_out=den_s[p][:, 0:1]).then_inc(de_ready, 1)
                    act.wait_ge(dnm_ready, 3 * b + 3)
                    sb = s[:, CA + FR:CA + FR + CB + FR]
                    act.activation(sb, sb, ACT.Exp, bias=nm_s[p][:, 1:2],
                                   accum_out=den_s[p][:, 1:2]).then_inc(de_ready, 1)
                    act.activation(es_s[p], sd_s[p], ACT.Exp).then_inc(de_ready, 1)
                    act.wait_ge(dpT_psum, b + 1)
                    act.copy(pT[p][:, 0:2, :].rearrange("p a b -> p (a b)"), PS[:, 4, 0:2 * P]).then_inc(dpT_ready, 1)
                    act.copy(pT[p][0:FR, 2, :], PS[0:FR, 4, 2 * P:3 * P]).then_inc(dpT_ready, 1)
                    act.copy(pT[p][:, 3, :], PS[:, 5, 0:P]).then_inc(dpT_ready, 1)
                    act.copy(pT[p][0:FR, 4, :], PS[0:FR, 5, P:2 * P]).then_inc(dpT_ready, 1)

                with act.Fori(0, STREAMS // 2) as i:
                    for p in range(2):
                        stream(2 * i + p, p)
                out_squares(NT_PROMPT)

            @block.vector
            def _(dve):
                ch = Chain(dve, dve_chain)

                def norm(t, p):
                    dve.wait_ge(rms_ready, t + 1)
                    invert_rms(dve, ch, rstd[:, 0:1], ss[:, 0:1], newton[:, :, 0:1], D)
                    dve.tensor_scalar(xn, x_sb[p], rstd[:, 0:1], None, ALU.mult).then_inc(xn_ready, 1)

                def piece(t, k):
                    if k < 2:
                        dve.wait_ge(xT_psum, 2 * t + k + 1)
                        dve.tensor_tensor(xT[:, 4 * k:4 * k + 4, :], PS[:, UNIT, :].rearrange("p (b c) -> p b c", c=P),
                                          gcol(g1_sb[:, 4 * k:4 * k + 4], 4), ALU.mult).then_inc(xT_ready, 1)

                def merge(t, p):
                    dve.wait_ge(rmso_ready, t + 1)
                    invert_rms(dve, ch, rstd[:, 1:3], ss[:, 1:3], newton, AW)
                    dve.tensor_scalar(o_sb[:, 0:AW], o_sb[:, 0:AW], rstd[:, 1:2], None, ALU.mult).then_inc(on_ready, 1)
                    dve.tensor_scalar(o_sb[:, AW:D], o_sb[:, AW:D], rstd[:, 2:3], None, ALU.mult).then_inc(on_ready, 1)
                    dve.wait_ge(oT_psum, t + 1)
                    dve.tensor_tensor(oT, PS[:, 4:6, :].rearrange("p a (b c) -> p (a b) c", c=P), gcol(g_ab_sb, KD),
                                      ALU.mult).then_inc(oT_ready, 1)
                    for c in range(2):
                        dve.wait_ge(wo_psum, 2 * t + c + 1)
                        cols = slice(512 * c, 512 * c + 512)
                        dve.tensor_tensor(x_sb[p][:, cols], PS[:, 6 + c, :], x_sb[p][:, cols],
                                          ALU.add).then_inc(h_ready, 1)

                def item(t, n):
                    q = n % 2
                    h = n % H
                    dve.wait_ge(s_psum, 16 * t + n + 1)
                    if n >= 2:
                        dve.wait_ge(pT_psum, 16 * t + n - 1)
                    elif n == 0:
                        dve.wait_ge(sso_ready, 2 * t + CREDIT)
                    if n < H:
                        dve.tensor_copy(sc[q][:, 4 * P:A_KEYS], PS[:, S_OWN, 0:P]).then_inc(s_read, 1)
                        dve.tensor_tensor(sc[q][:, 0:4 * P], PS[:, S_BANK[q], :], valid[:, 0:4 * P], ALU.add)\
                           .then_inc(s_read, 1)
                        s, bias, floor = sc[q], bias_a_sb[:, h, :], LOWEST
                    else:
                        s, bias, floor = sc[q][:, 0:B_KEYS], bias_b_sb[:, h, :], sink_sb[:, h:h + 1]
                        dve.tensor_tensor(s, PS[:, S_BANK[q], 0:B_KEYS], valid[:, A_KEYS - B_KEYS:A_KEYS],
                                          ALU.add).then_inc(s_read, 1)
                    dve.wait_ge(s_read, TILE_PARTS * t + item_parts(n))
                    ch.pass_on()
                    ch.mark(dve.tensor_tensor_reduce(s, s, bias, 1.0, floor, ALU.add, ALU.max, m_sb[:, n:n + 1]))
                    ch.settle()
                    dve.tensor_scalar(nm[:, n:n + 1], m_sb[:, n:n + 1], -1.0, None, ALU.mult)\
                       .then_inc(nm_ready, 1)

                dve.wait_ge(g1_in, 16)
                norm(0, 0)
                for k in PIECES:
                    piece(0, k)
                ch.restart()
                dve.wait_ge(const_in, 16 * 7)
                dve.wait_ge(windows_clear, 2)
                with dve.Fori(0, NT_PROMPT // 2) as i:
                    for p in range(2):
                        t = 2 * i + p
                        dve.wait_ge(shifted, t + 1 + CREDIT)
                        for n in range(16):
                            item(t, n)
                            if n == NORM_AT:
                                norm(t + 1, 1 - p)
                            if n - 1 in PIECE_AT:
                                piece(t + 1, PIECE_AT[n - 1])
                        dve.wait_ge(nm_ready, 16 * t + 16)
                        dve.tensor_tensor(sd, nm[:, H:16], sink_sb[:, 0:H], ALU.add).then_inc(sd_ready, 1)
                        dve.wait_ge(es_ready, t + 1)
                        ch.mark(dve.tensor_tensor(den[:, H:16], den[:, H:16], es, ALU.add))
                        ch.settle()
                        ch.mark(dve.reciprocal(rcp, den))
                        ch.settle()
                        dve.wait_ge(o_psum, 16 * t + 16 + CREDIT)
                        for g, bank in enumerate((OA_BANK, OB_BANK)):
                            dve.tensor_tensor(
                                o_sb[:, AW * g:AW * (g + 1)].rearrange("p (h d) -> p h d", h=H),
                                PS[:, bank, :].rearrange("p (h d) -> p h d", h=H),
                                rcp[:, H * g:H * (g + 1)].unsqueeze(2).broadcast_to([P, H, HD]), ALU.mult)\
                               .then_inc(o_ready, 1)
                        merge(t, p)
                        ch.restart()

                def expand(b, p):
                    fr = bass.ds(b * FR, FR)
                    qx = qx_sb[p].rearrange("p (j c) -> p j c", j=4)
                    dve.tensor_copy(qx[0:64, :, 0:FR], qT[0:64, 0:4, fr]).then_inc(qx_ready, 1)
                    dve.tensor_copy(qx[64:P, :, FR:2 * FR], qT[64:P, 0:4, fr]).then_inc(qx_ready, 1)
                    qxb = qxb_sb[p].rearrange("p (n g f) -> p n g f", n=2, g=4)
                    dve.tensor_copy(qxb[0:64, 0], qT[0:64, 4:8, fr]).then_inc(qx_ready, 1)
                    dve.tensor_copy(qxb[64:P, 1], qT[64:P, 4:8, fr]).then_inc(qx_ready, 1)

                def collect(b):
                    fr = bass.ds(b * FR, FR)
                    dve.wait_ge(doT_psum, b + 1)
                    oa = PS[:, 6, :].rearrange("p (j c) -> p j c", j=4)
                    ob = PS[:, 7, 0:P].rearrange("p (n g f) -> p n g f", n=2, g=4)
                    dve.tensor_copy(xT[0:64, 0:4, fr], oa[0:64, :, 0:FR]).then_inc(doT_ready, 1)
                    dve.tensor_copy(xT[64:P, 0:4, fr], oa[64:P, :, FR:2 * FR]).then_inc(doT_ready, 1)
                    dve.tensor_copy(xT[0:64, 4:8, fr], ob[0:64, 0]).then_inc(doT_ready, 1)
                    dve.tensor_copy(xT[64:P, 4:8, fr], ob[64:P, 1]).then_inc(doT_ready, 1)

                def stream(b, p, first=False, last=False):
                    cols = (slice(0, CA + FR), slice(CA + FR, CA + FR + CB + FR))
                    for g, (bias, floor) in enumerate(((bias_sa_sb, LOWEST), (bias_sb_sb, sink_sb[:, H:H + 1]))):
                        dve.wait_ge(ds_psum, 2 * b + g + 1 + CREDIT)
                        ch.pass_on()
                        keys = cols[g].stop - cols[g].start
                        ch.mark(dve.tensor_tensor_reduce(sc[p][:, cols[g]], PS[:, 2 * g + p, 0:keys], bias,
                                                         1.0, floor, ALU.add, ALU.max, m_s[p][:, g:g + 1]))
                        ch.settle()
                        dve.tensor_scalar(nm_s[p][:, g:g + 1], m_s[p][:, g:g + 1], -1.0, None, ALU.mult)\
                           .then_inc(dnm_ready, 1)
                    dve.wait_ge(dnm_ready, 3 * b + 2)
                    dve.tensor_tensor(sd_s[p], nm_s[p][:, 1:2], sink_sb[:, H:H + 1], ALU.add)\
                       .then_inc(dnm_ready, 1)
                    if not last:
                        expand(b + 1, 1 - p)
                    if not first:
                        collect(b - 1)
                    dve.wait_ge(de_ready, 3 * b + 3)
                    ch.mark(dve.tensor_tensor(den_s[p][:, 1:2], den_s[p][:, 1:2], es_s[p], ALU.add))
                    ch.settle()
                    ch.mark(dve.reciprocal(rcp_s[p], den_s[p]))
                    ch.settle()
                    for g in range(2):
                        dve.tensor_scalar(sc[p][:, cols[g]], sc[p][:, cols[g]], rcp_s[p][:, g:g + 1], None,
                                          ALU.mult).then_inc(dp_ready, 1)
                    ch.restart()

                dve.wait_ge(qkT_ready, 4 * NT_PROMPT + 4)
                dve.wait_ge(qx_clear, 4)
                expand(0, 0)
                stream(0, 0, first=True)
                stream(1, 1)
                with dve.Fori(1, STREAMS // 2 - 1) as i:
                    for p in range(2):
                        stream(2 * i + p, p)
                stream(6, 0)
                stream(7, 1, last=True)
                collect(7)
                dve.wait_ge(do_psum, 1)
                dve.tensor_copy(o_sb[:, 0:AW], PS[:, 0, :]).then_inc(o_ready, 1)
                dve.tensor_copy(o_sb[:, AW:D].rearrange("p (n g d) -> p g n d", n=2, g=4),
                                PS[:, 1, :].rearrange("p (g n d) -> p g n d", n=2, g=4)).then_inc(o_ready, 1)
                merge(NT_PROMPT, 0)

            @block.tensor
            def _(pe):
                def tr(bank, k, src):
                    return pe.transpose(PS[:, bank, k * P:(k + 1) * P], src, ident)

                def piece(t, k):
                    if k < 2:
                        if k == 0:
                            pe.wait_ge(xn_ready, t + 1)
                        else:
                            pe.wait_ge(xT_ready, 2 * t + 1)
                        for j in range(4):
                            mm = tr(UNIT, j, xn[:, (4 * k + j) * P:(4 * k + j + 1) * P])
                        mm.then_inc(xT_psum, 1)
                        return
                    c = BLOCKS[k - 2]
                    pe.wait_ge(w_in_in[c], 16)
                    if k == 2:
                        pe.wait_ge(xT_ready, 2 * t + 2)
                    else:
                        pe.wait_ge(z_ready, 5 * t + k - 2)
                    w = min(512, W_IN - 512 * c)
                    for j in range(KD):
                        mm = pe.matmul(PS[:, UNIT, 0:w], xT[:, j, :], w_in_sb[:, j, 512 * c:512 * c + w],
                                       start=(j == 0), stop=(j == KD - 1))
                    mm.then_inc(proj_psum, 1)

                def turn_qk(t):
                    pe.wait_ge(z_ready, 5 * t + 4)
                    for bank, z0, n in ((0, 0, 4), (2, 3 * AW, 4), (1, AW, 4), (3, 4 * AW, 1)):
                        for k in range(n):
                            mm = tr(bank, k, z[:, z0 + k * P:z0 + (k + 1) * P])
                        mm.then_inc(qkT_psum, 1)

                def scores(t, n):
                    q = n % 2
                    if n >= 2:
                        pe.wait_ge(s_read, TILE_PARTS * t + item_parts(n - 2))
                    if n < H:
                        rows = slice(64 * (n % 2), 64 * (n % 2) + 64)
                        mm = pe.matmul(PS[:, S_BANK[q], :], qT[rows, n // 2, :], k_win[rows, n // 2, 0:4 * P],
                                       start=True, stop=True)
                        if n:
                            pe.wait_ge(s_read, TILE_PARTS * t + item_parts(n - 1) - 1)
                        mm = pe.matmul(PS[:, S_OWN, 0:P], qT[rows, n // 2, :], k_win[rows, n // 2, 4 * P:A_KEYS],
                                       start=True, stop=True)
                    else:
                        kv, g = (n - H) // 4, (n - H) % 4
                        rows = slice(64 * kv, 64 * kv + 64)
                        mm = pe.matmul(PS[:, S_BANK[q], 0:B_KEYS], qT[rows, 4 + g, :], kb_win[rows, :],
                                       start=True, stop=True)
                    mm.then_inc(s_psum, 1)

                def turn(t, n):
                    q = n % 2
                    pe.wait_ge(e_ready, 16 * t + n + 1)
                    if n >= 2:
                        pe.wait_ge(pT_ready, TILE_PARTS * t + item_parts(n - 2))
                    for k in range(A_BLK if n < H else 2):
                        if k == 4 and n:
                            pe.wait_ge(pT_ready, TILE_PARTS * t + item_parts(n - 1) - 1)
                        mm = tr(PT_BANK[q] if k < 4 else PT_OWN, k % 4, sc[q][:, k * P:(k + 1) * P])
                    mm.then_inc(pT_psum, 1)

                def weigh(t, n):
                    pe.wait_ge(pT_ready, TILE_PARTS * t + item_parts(n))
                    if n < H:
                        cols = slice(n * HD, min(n + 2, H) * HD)
                        for k in range(A_BLK):
                            mm = pe.matmul(PS[:, OA_BANK, cols], pT[n % 2][:, k, :],
                                           v_win[:, k, cols], start=(k == 0), stop=(k == A_BLK - 1))
                    else:
                        h = n - H
                        kv = h // 4
                        for k in range(2):
                            mm = pe.matmul(PS[:, OB_BANK, h * HD:(h + 1) * HD], pT[n % 2][:, k, :],
                                           vb_win[:, k, kv * HD:(kv + 1) * HD], start=(k == 0), stop=(k == 1))
                    mm.then_inc(o_psum, 1)

                def out_project(t, next_t):
                    pe.wait_ge(on_ready, 2 * t + 2)
                    for k in range(KD):
                        mm = tr(4 + k // 4, k % 4, o_sb[:, k * P:(k + 1) * P])
                    mm.then_inc(oT_psum, 1)
                    pe.wait_ge(oT_ready, t + 1)
                    for c in range(2):
                        if c:
                            pe.wait_ge(z_ready, 5 * next_t + 5)
                        for k in range(KD):
                            mm = pe.matmul(PS[:, 6 + c, :], oT[:, k, :], w_out_sb[:, k, 512 * c:512 * c + 512],
                                           start=(k == 0), stop=(k == KD - 1))
                        mm.then_inc(wo_psum, 1)

                pe.wait_ge(ident_ready, 2)
                for k in PIECES:
                    piece(0, k)
                turn_qk(0)
                with pe.Fori(0, NT_PROMPT) as t:
                    pe.wait_ge(qkT_ready, 4 * t + 4)
                    scores(t, 0)
                    scores(t, 1)
                    pe.wait_ge(shifted, t + 1 + CREDIT)
                    pe.wait_ge(h_ready, 2 * t + CREDIT)
                    for n in range(16):
                        turn(t, n)
                        if n + 2 < 16:
                            scores(t, n + 2)
                        if n:
                            weigh(t, n - 1)
                        if n in PIECE_AT:
                            piece(t + 1, PIECE_AT[n])
                    weigh(t, 15)
                    turn_qk(t + 1)
                    piece(t + 1, LAST_PIECE)
                    pe.wait_ge(w_out_in, 16)
                    out_project(t, t + 1)

                def stream_scores(b, p, i):
                    pe.wait_ge(cache_k_in[p], 32 * i + 32)
                    pe.wait_ge(qx_ready, 4 * b + 4)
                    new = bass.ds(A_KEYS - P + b * FR, FR)
                    for keys, rhs in ((slice(0, CA), lambda j: ckT_sb[p][:, j, :]),
                                      (slice(CA, CA + FR), lambda j: k_win[:, j, new])):
                        for j in range(4):
                            mm = pe.matmul(PS[:, p, keys], qx_sb[p][:, j * P:(j + 1) * P], rhs(j),
                                           start=(j == 0), stop=(j == 3))
                    mm.then_inc(ds_psum, 1)
                    pe.matmul(PS[:, 2 + p, 0:CB], qxb_sb[p], ckbT_sb[p], start=True, stop=True)
                    pe.matmul(PS[:, 2 + p, CB:CB + FR], qxb_sb[p], kb_win[:, bass.ds(P + b * FR, FR)],
                              start=True, stop=True).then_inc(ds_psum, 1)

                def stream_values(b, p, i):
                    pe.wait_ge(cache_v_in[p], 64 * i + 64)
                    pe.wait_ge(dp_ready, 2 * b + 2)
                    pe.wait_ge(dpT_ready, 4 * b + CREDIT)
                    tr(4, 0, sc[p][:, 0:P])
                    tr(4, 1, sc[p][:, P:CA])
                    pe.transpose(PS[0:FR, 4, 2 * P:3 * P], sc[p][:, CA:CA + FR], ident)
                    tr(5, 0, sc[p][:, CA + FR:CA + FR + CB])
                    pe.transpose(PS[0:FR, 5, P:2 * P], sc[p][:, CA + FR + CB:CA + CB + 2 * FR], ident)\
                      .then_inc(dpT_psum, 1)
                    pe.wait_ge(dpT_ready, 4 * b + 4 + CREDIT)
                    pe.wait_ge(doT_ready, 4 * b + CREDIT)
                    for j in range(4):
                        out = PS[:, 6, 96 * j:96 * j + P]
                        w = slice(j * P, (j + 1) * P)
                        for k in range(2):
                            pe.matmul(out, cv_sb[p][:, k, w], pT[p][:, k, :], start=(k == 0), stop=False)
                        pe.matmul(out, vnew_sb[p][0:FR, w], pT[p][0:FR, 2, :], start=False, stop=True)
                    pe.matmul(PS[:, 7, 0:P], cvb_sb[p], pT[p][:, 3, :], start=True, stop=False)
                    pe.matmul(PS[:, 7, 0:P], vnew_sb[p][0:FR, AW:AW + P], pT[p][0:FR, 4, :],
                              start=False, stop=True).then_inc(doT_psum, 1)

                pe.wait_ge(qkT_ready, 4 * NT_PROMPT + 4)
                stream_scores(0, 0, 0)
                pe.wait_ge(h_ready, 2 * NT_PROMPT + CREDIT)
                with pe.Fori(0, STREAMS // 2 - 1) as i:
                    stream_scores(2 * i + 1, 1, i)
                    stream_values(2 * i, 0, i)
                    stream_scores(2 * i + 2, 0, i + 1)
                    stream_values(2 * i + 1, 1, i)
                stream_scores(7, 1, 3)
                stream_values(6, 0, 3)
                stream_values(7, 1, 3)
                pe.wait_ge(doT_ready, 4 * STREAMS + CREDIT)
                for k in range(KD):
                    mm = tr(k // 4, k % 4, xT[:, k, :])
                mm.then_inc(do_psum, 1)
                out_project(NT_PROMPT, NT_PROMPT)

        top[0] = shared_top
        uv = [carve(2 * D) for _ in range(RING)]
        x2 = [carve(D) for _ in range(2)]
        hb = [carve(D) for _ in range(2)]
        x2T = carve(KD, P)
        qT2 = carve(2 * QSP, P)
        s_sb = carve(16, P)
        s_left = carve(P)
        g2_bc = carve(D)
        gf_bc = carve(D)
        y_sb = carve(D)
        diag = carve(RING, P)
        rank = carve(CAND)
        onehot = carve(QSP * TOPK, CAND)
        sv = carve(16, TOPK)
        si_u = carve(16, TOPK).bitcast(U32)
        si = carve(16, TOPK)
        cand = carve(H, CAND)
        expert_of = carve(H, CAND)
        c_left = carve(CAND)
        fv = carve(H, TOPK)
        fi_u = carve(H, TOPK).bitcast(U32)
        fi = carve(H, TOPK)
        eidx = carve(SLOTS)
        expert_idx = [carve(SLOTS).bitcast(U32) for _ in range(2)]
        gate = [carve(SLOTS) for _ in range(2)]
        gden = carve(H)
        a_dot = [carve(GROUP) for _ in range(2)]
        a_gelu = [carve(GROUP) for _ in range(2)]
        wgt = [carve(GROUP) for _ in range(2)]
        ss2 = carve(2)
        rstd2 = carve(2)
        newton2 = carve(2, 1)

        bc_in = sem("bc_in")
        h_in = [sem(f"h_in{p}") for p in range(2)]
        rank_ready = sem("rank_ready")
        chain_b = sem("chain_b")
        gather_chain = sem("gather_chain")
        ss2_ready = sem("ss2_ready")
        rms2_ready = sem("rms2_ready")
        x2_ready = sem("x2_ready")
        x2T_psum = sem("x2T_psum")
        x2T_ready = sem("x2T_ready")
        q_psum = sem("q_psum")
        q_ready = sem("q_ready")
        key_psum = sem("key_psum")
        key_ready = sem("key_ready")
        g_shift = sem("g_shift")
        g_exp = sem("g_exp")
        routed = sem("routed")
        uv_in = [sem(f"uv_in{s}") for s in range(RING)]
        dots_ready = sem("dots_ready")
        gelu_ready = sem("gelu_ready")
        wgt_ready = sem("wgt_ready")
        diag_ready = sem("diag_ready")
        slot_used = sem("slot_used")
        ssf_ready = sem("ssf_ready")
        rmsf_ready = sem("rmsf_ready")
        opened = sem("opened")
        y_ready = sem("y_ready")
        y_stored = sem("y_stored")

        def pieces(run, route_part, finish):
            def tiles(t, u, p, more):
                for part in range(AHEAD, PARTS):
                    if more:
                        for step, *pairs in ROUTE_AT[part]:
                            route_part(t + 1, u + p, 1 - p, step, *pairs)
                    run(t, p, part)
                if more:
                    run(t + 1, 1 - p, 0)
                finish(t, p)
                if more:
                    for part in range(1, AHEAD):
                        run(t + 1, 1 - p, part)

            def first():
                for item in FIRST:
                    if isinstance(item, int):
                        run(0, 0, item)
                    else:
                        step, *pairs = item
                        route_part(0, 0, 0, step, *pairs)
            return first, tiles

        def gate_turn(t, k):
            return k + 1 if isinstance(t, int) and t == 0 else t + PAIRS

        with nc.Block() as block:

            @block.sync
            def _(sp):
                sp.dma_start(hb[0], h_dram[0:P, :]).then_inc(h_in[0], 16)
                sp.dma_start(g2_bc, g2[0:1, :].broadcast_to([P, D])).then_inc(bc_in, 16)
                sp.dma_start(gf_bc, gf[0:1, :].broadcast_to([P, D])).then_inc(bc_in, 16)
                sp.dma_start(hb[1], h_dram[P:2 * P, :]).then_inc(h_in[1], 16)

                def load_h(t, p):
                    sp.wait_ge(opened, t - 1)
                    sp.dma_start(hb[p], h_dram[bass.ds(t * P, P), :]).then_inc(h_in[p], 16)

                def store(t, dst):
                    sp.wait_ge(y_ready, t + 1 + Y_CREDIT)
                    sp.dma_start(dst, y_sb).then_inc(y_stored, 16)

                with sp.Fori(0, 3) as i:
                    for p in range(2):
                        t = 2 * i + p
                        load_h(t + 2, p)
                        store(t, y_p[bass.ds(t * P, P), :])
                load_h(NT_PROMPT, 0)
                store(6, y_p[6 * P:7 * P, :])
                store(7, y_p[7 * P:8 * P, :])
                store(NT_PROMPT, y_s)
                sp.wait_ge(y_stored, 16 * NT + 16 * CREDIT)

            @block.gpsimd
            def _(pool):
                pool.sem_inc(y_stored, 16 * CREDIT)
                pool.sem_inc(y_ready, Y_CREDIT)
                pool.iota(rank, pattern=[[1, CAND]], base=0, channel_multiplier=0,
                          allow_small_or_imprecise_dtypes=True).then_inc(rank_ready, 1)

                ch = Chain(pool, gather_chain)

                def gathers(t, p):
                    for s in range(SLOTS):
                        r = s % RING
                        if s % (QSP * TOPK) == 0:
                            pool.wait_ge(routed, PAIRS * t + s // (QSP * TOPK) + 1)
                            ch.pass_on()
                        if s >= RING or not isinstance(t, int) or t > 0:
                            pool.wait_ge(slot_used, t * SLOTS + s - RING + 1)
                            ch.pass_on()
                        pool.indirect_dma_start(
                            out=uv[r], out_offset=None, in_=experts,
                            in_offset=bass.IndirectOffsetOnAxis(ap=expert_idx[p][:, s:s + 1], axis=0))\
                            .then_inc(uv_in[r], 16)
                    ch.restart()

                gathers(0, 0)
                gathers(1, 1)
                with pool.Fori(1, 4) as i:
                    for p in range(2):
                        gathers(2 * i + p, p)
                gathers(NT_PROMPT, 0)

            @block.scalar
            def _(act):
                def run(t, p, part):
                    for g in range(PER_PART // GROUP):
                        n = part * (PER_PART // GROUP) + g
                        q = n % 2
                        grp = t * (SLOTS // GROUP) + n
                        act.wait_ge(dots_ready, grp * GROUP + GROUP)
                        act.activation(a_gelu[q], a_dot[q], ACT.Gelu).then_inc(gelu_ready, 1)
                        act.wait_ge(wgt_ready, grp + 1)
                        for k in range(GROUP):
                            s = n * GROUP + k
                            if s >= RING or not isinstance(t, int) or t > 0:
                                act.wait_ge(slot_used, t * SLOTS + s - RING + 1)
                            act.activation(diag[:, s % RING, :], ident, ACT.Copy,
                                           scale=wgt[q][:, k:k + 1]).then_inc(diag_ready, 1)

                def route_part(t, u, p, step, k, n=1):
                    if step == "keys" and k == 0:
                        act.wait_ge(h_in[p], 16 * u + 16)
                        act.activation(x2[p], hb[p], ACT.Square, accum_out=ss2[:, 0:1]).then_inc(ss2_ready, 1)
                        act.wait_ge(ss2_ready, t + 1)
                        act.activation(rstd2[:, 0:1], ss2[:, 0:1], ACT.Sqrt, bias=eps, scale=1.0 / D)\
                           .then_inc(rms2_ready, 1)
                        act.wait_ge(x2T_psum, t + 1)
                        act.copy(x2T.rearrange("p a b -> p (a b)"), PS[:, 4:6, :].rearrange("p a b -> p (a b)"))\
                           .then_inc(x2T_ready, 1)
                    if step == "keys":
                        act.wait_ge(q_psum, 4 * t + k + 1)
                        act.copy(qT2.rearrange("p a b -> p (a b)"), PS[:, 6, :]).then_inc(q_ready, 1)
                        act.wait_ge(key_psum, 4 * t + k + 1)
                        act.copy(s_sb[:, 4 * k:4 * k + 4, :].rearrange("p a b -> p (a b)"), PS[:, 7, :])\
                           .then_inc(key_ready, 1)
                    if step == "gates":
                        act.wait_ge(g_shift, gate_turn(t, k))
                        g = gate[p][:, QSP * TOPK * k:QSP * TOPK * (k + n)]
                        act.activation(g, g, ACT.Exp).then_inc(g_exp, 1)

                def finish(t, p):
                    act.wait_ge(slot_used, (t + 1) * SLOTS)
                    act.wait_ge(y_stored, 16 * t + 16 * CREDIT)
                    act.activation(y_sb, PS[:, 2 * p:2 * p + 2, :].rearrange("p a b -> p (a b)"), ACT.Square,
                                   accum_out=ss2[:, 1:2]).then_inc(ssf_ready, 1)
                    act.wait_ge(ssf_ready, t + 1)
                    act.activation(rstd2[:, 1:2], ss2[:, 1:2], ACT.Sqrt, bias=eps, scale=1.0 / D)\
                       .then_inc(rmsf_ready, 1)

                first, tiles = pieces(run, route_part, finish)
                first()
                with act.Fori(0, 4) as i:
                    for p in range(2):
                        tiles(2 * i + p, i, p, True)
                tiles(NT_PROMPT, NT_PROMPT // 2, 0, False)

            @block.vector
            def _(dve):
                ch = Chain(dve, chain_b)

                def run(t, p, part):
                    for g in range(PER_PART // GROUP):
                        n = part * (PER_PART // GROUP) + g
                        q = n % 2
                        for k in range(GROUP):
                            s = n * GROUP + k
                            r = s % RING
                            dve.wait_ge(uv_in[r], 16 * (t * (SLOTS // RING) + s // RING + 1))
                            dve.tensor_tensor_reduce(uv[r][:, 0:D], uv[r][:, 0:D], x2[p], 1.0, 0.0, ALU.mult,
                                                     ALU.add, a_dot[q][:, k:k + 1])\
                               .then_inc(dots_ready, 1)
                        grp = t * (SLOTS // GROUP) + n
                        dve.wait_ge(gelu_ready, grp + 1)
                        dve.tensor_tensor(wgt[q], a_gelu[q], gate[p][:, n * GROUP:(n + 1) * GROUP], ALU.mult)\
                           .then_inc(wgt_ready, 1)

                def top16(values, left, src, idx):
                    ch.mark(dve.max(values[:, 0:8], src))
                    ch.settle()
                    ch.mark(dve.match_replace(left, values[:, 0:8], src, LOWEST))
                    ch.mark(dve.max_index(idx[:, 0:8], values[:, 0:8], src))
                    ch.settle()
                    ch.mark(dve.max(values[:, 8:16], left))
                    ch.settle()
                    ch.mark(dve.max_index(idx[:, 8:16], values[:, 8:16], left))

                def route_part(t, u, p, step, k, n=1):
                    hs = slice(QSP * k, QSP * (k + n))
                    if step == "keys" and k == 0:
                        dve.wait_ge(rms2_ready, t + 1)
                        invert_rms(dve, ch, rstd2[:, 0:1], ss2[:, 0:1], newton2, D)
                        dve.scalar_tensor_tensor(out=x2[p], in0=hb[p], scalar=rstd2[:, 0:1], in1=g2_bc,
                                                 op0=ALU.mult, op1=ALU.mult).then_inc(x2_ready, 1)
                    if step == "halves":
                        dve.wait_ge(key_ready, 4 * t + k + 1)
                        ch.pass_on()
                        for l in range(4 * k, 4 * k + 4):
                            top16(sv[:, l, :], s_left, s_sb[:, l, :], si_u[:, l, :])
                        ch.settle()
                    if step == "sums":
                        ch.mark(dve.tensor_copy(si[:, 4 * k:4 * k + 4, :], si_u[:, 4 * k:4 * k + 4, :]))
                        ch.settle()
                        si4 = si.rearrange("p (h two) k -> p h two k", two=2)
                        sv4 = sv.rearrange("p (h two) k -> p h two k", two=2)
                        ch.mark(dve.tensor_scalar(si4[:, hs, 0, :], si4[:, hs, 0, :], float(NKEYS), None, ALU.mult))
                        ch.settle()
                        at = 0
                        for i, w in enumerate(ROWS):
                            if w == 1 and i and ROWS[i - 1] == 1:
                                continue
                            m = ROWS.count(1) if w == 1 else 1
                            for dst, v4 in ((cand, sv4), (expert_of, si4)):
                                if w == 1:
                                    a = v4[:, hs, 0, i:i + m]
                                    b = v4[:, hs, 1, 0:1].broadcast_to([P, QSP, m])
                                else:
                                    a = v4[:, hs, 0, i:i + 1].broadcast_to([P, QSP, w])
                                    b = v4[:, hs, 1, 0:w]
                                ch.mark(dve.tensor_tensor(dst[:, hs, at:at + w * m], a, b, ALU.add))
                            at += w * m
                        assert at == CAND
                        ch.settle()
                        for h in range(QSP * k, QSP * (k + 1)):
                            top16(fv[:, h, :], c_left, cand[:, h, :], fi_u[:, h, :])
                        ch.settle()
                    if step == "experts":
                        ch.mark(dve.tensor_copy(fi[:, hs, :], fi_u[:, hs, :]))
                        ch.settle()
                        oh = onehot.rearrange("p (h k) c -> p h k c", h=QSP)
                        for h in range(QSP):
                            ch.mark(dve.tensor_tensor(
                                oh[:, h], rank.unsqueeze(1).broadcast_to([P, TOPK, CAND]),
                                fi[:, QSP * k + h, :].unsqueeze(2).broadcast_to([P, TOPK, CAND]), ALU.is_equal))
                        ch.settle()
                        for h in range(QSP):
                            ch.mark(dve.tensor_tensor(
                                oh[:, h], oh[:, h],
                                expert_of[:, QSP * k + h, :].unsqueeze(1).broadcast_to([P, TOPK, CAND]), ALU.mult))
                        ch.settle()
                        ks = slice(QSP * TOPK * k, QSP * TOPK * (k + 1))
                        ch.mark(dve.tensor_reduce(eidx[:, ks], onehot, AX_X, ALU.add))
                        ch.settle()
                        dve.tensor_copy(expert_idx[p][:, ks], eidx[:, ks]).then_inc(routed, 1)
                    if step == "gates":
                        g3 = gate[p].rearrange("p (h k) -> p h k", h=H)[:, hs, :]
                        d = gden[:, hs]
                        dve.tensor_tensor(g3, fv[:, hs, :], fv[:, hs, 0:1].broadcast_to([P, QSP * n, TOPK]),
                                          ALU.subtract).then_inc(g_shift, 1)
                        dve.wait_ge(g_exp, gate_turn(t, k))
                        ch.mark(dve.tensor_reduce(d, g3, AX_X, ALU.add))
                        ch.settle()
                        ch.mark(dve.reciprocal(d, d))
                        ch.settle()
                        ch.mark(dve.tensor_tensor(g3, g3, d.unsqueeze(2).broadcast_to([P, QSP * n, TOPK]), ALU.mult))
                        ch.restart()

                def finish(t, p):
                    dve.wait_ge(rmsf_ready, t + 1)
                    invert_rms(dve, ch, rstd2[:, 1:2], ss2[:, 1:2], newton2, D)
                    ch.restart()
                    dve.scalar_tensor_tensor(out=y_sb, in0=PS[:, 2 * p:2 * p + 2, :].rearrange("p a b -> p (a b)"),
                                             scalar=rstd2[:, 1:2], in1=gf_bc, op0=ALU.mult, op1=ALU.mult)\
                       .then_inc(y_ready, 1)

                dve.wait_ge(bc_in, 32)
                dve.wait_ge(rank_ready, 1)
                first, tiles = pieces(run, route_part, finish)
                first()
                with dve.Fori(0, 4) as i:
                    for p in range(2):
                        tiles(2 * i + p, i, p, True)
                tiles(NT_PROMPT, NT_PROMPT // 2, 0, False)

            @block.tensor
            def _(pe):
                def run(t, p, part):
                    if part == 0:
                        pe.wait_ge(y_ready, t - 1 + Y_CREDIT)
                        for c in range(2):
                            mm = pe.matmul(PS[:, 2 * p + c, :], ident, hb[p][:, 512 * c:512 * c + 512],
                                           start=True, stop=False)
                        mm.then_inc(opened, 1)
                    for s in range(part * PER_PART, (part + 1) * PER_PART):
                        r = s % RING
                        pe.wait_ge(diag_ready, t * SLOTS + s + 1)
                        for c in range(2):
                            mm = pe.matmul(PS[:, 2 * p + c, :], diag[:, r, :],
                                           uv[r][:, D + 512 * c:D + 512 * c + 512], start=False,
                                           stop=(s == SLOTS - 1))
                        mm.then_inc(slot_used, 1)

                def route_part(t, u, p, step, k, n=1):
                    if step == "keys" and k == 0:
                        pe.wait_ge(x2_ready, t + 1)
                        for j in range(KD):
                            mm = pe.transpose(PS[:, 4 + j // 4, (j % 4) * P:(j % 4 + 1) * P],
                                              x2[p][:, j * P:(j + 1) * P], ident)
                        mm.then_inc(x2T_psum, 1)
                        pe.wait_ge(x2T_ready, t + 1)
                    if step == "keys":
                        for l in range(4):
                            c = (4 * k + l) * P
                            for j in range(KD):
                                mm = pe.matmul(PS[:, 6, l * P:(l + 1) * P], w_query_sb[:, j, c:c + P], x2T[:, j, :],
                                               start=(j == 0), stop=(j == KD - 1))
                        mm.then_inc(q_psum, 1)
                        pe.wait_ge(q_ready, 4 * t + k + 1)
                        for l in range(4):
                            mm = pe.matmul(PS[:, 7, l * P:(l + 1) * P], qT2[:, l, :], subk_sb[:, 4 * k + l, :],
                                           start=True, stop=True)
                        mm.then_inc(key_psum, 1)

                def finish(t, p):
                    pass

                pe.wait_ge(w_query_ready, 16 * (KD + 1))
                first, tiles = pieces(run, route_part, finish)
                first()
                with pe.Fori(0, 4) as i:
                    for p in range(2):
                        tiles(2 * i + p, i, p, True)
                tiles(NT_PROMPT, NT_PROMPT // 2, 0, False)


def kernel(x_prompt, x_sample, cache_a_k, cache_a_v, cache_b_k, cache_b_v, norm1_g, w_in, rel_bias, sinks,
           out_norm_a_g, out_norm_b_g, w_out, norm2_g, w_query, sub_keys, expert_u, expert_v, norm_f_g):
    import numpy as np
    import concourse.bacc as bacc
    from concourse import mybir as mb
    from concourse.bass_utils import run_bass_kernel_spmd as run

    rel = np.asarray(rel_bias)[0]
    dist = 512 + np.arange(128)[:, None] - np.arange(640)[None, :]
    bias_a = rel[:, np.clip(dist, -63, 256) + 63].transpose(1, 0, 2)
    dist_s = 256 + np.arange(16)[:, None] - np.arange(272)[None, :]
    bias_sa = rel[:, np.clip(dist_s, -63, 256) + 63].reshape(128, 272)
    slope = 2.0 ** -np.arange(1, 9, dtype=np.float32)
    q, c = np.arange(128)[:, None], np.arange(256)[None, :]
    outside = (c // 64 < q // 64) | (c // 64 > q // 64 + 2)
    bias_b = np.where(outside[:, None, :], np.float32(-1e30),
                      -slope[None, :, None] * np.abs(128 + q - c).astype(np.float32)[:, None, :]).astype(np.float32)
    kpos = np.abs(128 + np.arange(16)[:, None] - np.arange(144)[None, :]).astype(np.float32)
    bias_sb = (-slope[:, None, None] * kpos[None]).reshape(128, 144).astype(np.float32)
    w = np.asarray(w_in)[0]
    qb = w[:, 1536:2048].reshape(1024, 2, 4, 64).transpose(0, 2, 1, 3).reshape(1024, 512)
    w = np.concatenate([w[:, :1536], qb, w[:, 2048:]], axis=1)
    ck = np.asarray(cache_a_k)[0].transpose(0, 2, 3, 1).reshape(8, 4, 128, 256).transpose(0, 2, 1, 3)
    arrays = {
        "x_prompt": np.asarray(x_prompt).reshape(1024, 1024),
        "x_sample": np.asarray(x_sample).reshape(128, 1024),
        "ckT": ck.reshape(1024, 1024),
        "cv": np.asarray(cache_a_v)[0].reshape(8 * 256, 512),
        "ckbT": np.asarray(cache_b_k)[0].transpose(0, 2, 3, 1).reshape(8 * 128, 128),
        "cvb": np.asarray(cache_b_v)[0].reshape(8 * 128, 128),
        "g1": np.asarray(norm1_g)[0].reshape(8, 128).T,
        "w_in": w,
        "bias_a": bias_a, "bias_b": bias_b, "bias_sa": bias_sa, "bias_sb": bias_sb,
        "sinks": np.asarray(sinks),
        "sink_rows": np.repeat(np.asarray(sinks)[0], 16).reshape(128, 1),
        "g_ab": np.concatenate([np.asarray(out_norm_a_g)[0], np.asarray(out_norm_b_g)[0]]).reshape(8, 128).T,
        "w_out": np.asarray(w_out)[0],
        "g2": np.asarray(norm2_g),
        "w_query": np.asarray(w_query)[0],
        "subk": np.asarray(sub_keys)[0].transpose(3, 0, 1, 2).reshape(128, 2048),
        "experts": np.concatenate([np.asarray(expert_u)[0], np.asarray(expert_v)[0]], axis=1),
        "gf": np.asarray(norm_f_g).reshape(1, 1024),
    }
    nc = bacc.Bacc("TRN2", target_bir_lowering=False, num_devices=1)
    ins, sent = [], {}
    for name, a in arrays.items():
        a = np.ascontiguousarray(a)
        sent[f"in_{name}"] = a
        ins.append(nc.dram_tensor(f"in_{name}", a.shape, mb.dt.from_np(a.dtype), kind="ExternalInput").ap())
    shapes = [(1024, 1024), (128, 1024), (512, 512), (512, 512), (128, 128), (128, 128),
              (128, 512), (128, 512), (128, 128), (128, 128)]
    outs = [nc.dram_tensor(f"out_{i}", s, mb.dt.float32, kind="ExternalOutput").ap() for i, s in enumerate(shapes)]
    build(nc, ins, outs)
    r = run(nc, [sent], core_ids=[0]).results[0]
    final = [(1, 1024, 1024), (8, 16, 1024), (1, 1, 512, 8, 64), (1, 1, 512, 8, 64), (1, 1, 128, 2, 64),
             (1, 1, 128, 2, 64), (1, 8, 16, 8, 64), (1, 8, 16, 8, 64), (1, 8, 16, 2, 64), (1, 8, 16, 2, 64)]
    return tuple(np.asarray(r[f"out_{i}"]).reshape(s) for i, s in enumerate(final))
```
